# Optimizing a Trainium2 kernel written in Bass

```python
import math
import jax, jax.numpy as jnp
from jax import lax
import numpy as np

D_MODEL = 1024
BATCH = 1
SEQ = 1024
DEPTH = 2
DEC_BATCH = 8
DEC_SEQ = 8
PAST_LEN = 8192
PAGE_SIZE = 128

N_HEADS = 4
DQK = D_MODEL // (2 * N_HEADS)
DV = D_MODEL // N_HEADS
QK_WIDTH = N_HEADS * DQK
V_WIDTH = N_HEADS * DV
GATE_RANK = 16
GATE_TAU = 16.0
D_FF = -(-8 * D_MODEL // (3 * 256)) * 256
CHUNK = 64
EPS = 1e-6
FORGET_BIAS = 3.0
N_MLSTM = (DEPTH + 1) // 2
N_GLA = DEPTH // 2
MLSTM_IN = 2 * QK_WIDTH + 2 * V_WIDTH + 2 * N_HEADS
GLA_IN = 2 * QK_WIDTH + 2 * V_WIDTH + GATE_RANK
SPLIT_MAIN = [QK_WIDTH, 2 * QK_WIDTH, 2 * QK_WIDTH + V_WIDTH, 2 * QK_WIDTH + 2 * V_WIDTH]

kernel_name = "hybrid_mlstm_gla_decoder_step"

def rms_norm(x, g):
    xf = x.astype(jnp.float32)
    y = xf * lax.rsqrt(jnp.mean(xf * xf, axis=-1, keepdims=True) + EPS)
    return (y * g.astype(jnp.float32)).astype(x.dtype)

def head_rms_norm(h, g):
    y = h * lax.rsqrt(jnp.mean(h * h, axis=-1, keepdims=True) + EPS)
    return y * g.astype(jnp.float32).reshape(N_HEADS, DV)

def _to_chunks(a, L):
    B, S = a.shape[:2]
    return jnp.moveaxis(a.reshape((B, S // L, L) + a.shape[2:]), 1, 0)

def _from_chunks(a):
    nc, B, L = a.shape[:3]
    return jnp.moveaxis(a, 0, 1).reshape((B, nc * L) + a.shape[3:])

def mlstm_chunked(q, k, v, i_pre, lf, C0, n0, m0):
    L = math.gcd(CHUNK, q.shape[1])
    causal = jnp.tril(jnp.ones((L, L), dtype=bool))

    def step(carry, inp):
        C, n, m = carry
        qc, kc, vc, ic, fc = inp
        b = jnp.cumsum(jnp.swapaxes(fc, 1, 2), axis=-1)
        ic = jnp.swapaxes(ic, 1, 2)
        D = jnp.where(causal, b[..., :, None] - b[..., None, :] + ic[..., None, :], -jnp.inf)
        inter = b + m[..., None]
        m_t = jnp.maximum(inter, jnp.max(D, axis=-1))
        w_inter = jnp.exp(inter - m_t)
        A = jnp.einsum('blhd,bshd->bhls', qc, kc) * jnp.exp(D - m_t[..., None])
        num = jnp.einsum('bhls,bshv->bhlv', A, vc) + w_inter[..., None] * jnp.einsum('blhd,bhdv->bhlv', qc, C)
        den = jnp.sum(A, axis=-1) + w_inter * jnp.einsum('blhd,bhd->bhl', qc, n)
        h = num / jnp.maximum(jnp.abs(den), jnp.exp(-m_t))[..., None]
        m_new = m_t[..., -1]
        w_s = jnp.exp(b[..., -1:] - b + ic - m_new[..., None])
        decay = jnp.exp(b[..., -1] + m - m_new)
        kw = kc * jnp.swapaxes(w_s, 1, 2)[..., None]
        C_new = decay[..., None, None] * C + jnp.einsum('bshd,bshv->bhdv', kw, vc)
        n_new = decay[..., None] * n + jnp.sum(kw, axis=1)
        return (C_new, n_new, m_new), jnp.swapaxes(h, 1, 2)

    xs = tuple(_to_chunks(a, L) for a in (q, k, v, i_pre, lf))
    carry0 = (C0.astype(jnp.float32), n0.astype(jnp.float32), m0.astype(jnp.float32))
    (C, n, m), h = lax.scan(step, carry0, xs)
    return _from_chunks(h), C, n, m

def gla_chunked(q, k, v, g, S0):
    L = math.gcd(CHUNK, q.shape[1])
    causal = jnp.tril(jnp.ones((L, L), dtype=bool))[None, :, :, None, None]

    def step(S, inp):
        qc, kc, vc, gc = inp
        Bc = jnp.cumsum(gc, axis=1)
        o_inter = jnp.einsum('blhd,bhdv->blhv', qc * jnp.exp(Bc), S)
        decay = jnp.exp(jnp.where(causal, Bc[:, :, None] - Bc[:, None, :], -jnp.inf))
        A = jnp.einsum('blhd,bshd,blshd->bhls', qc, kc, decay)
        o_intra = jnp.einsum('bhls,bshv->blhv', A, vc)
        BL = Bc[:, -1]
        S_new = jnp.exp(BL)[..., None] * S + jnp.einsum('bshd,bshv->bhdv', kc * jnp.exp(BL[:, None] - Bc), vc)
        return S_new, o_inter + o_intra

    xs = tuple(_to_chunks(a, L) for a in (q, k, v, g))
    S, o = lax.scan(step, S0.astype(jnp.float32), xs)
    return _from_chunks(o), S

def mlstm_mixer(x, w_in, b_i, b_f, g_head, w_out, C0, n0, m0):
    B, S, _ = x.shape
    proj = jnp.einsum('bsd,de->bse', x, w_in).astype(jnp.float32)
    q, k, v, o, ig, fg = jnp.split(proj, SPLIT_MAIN + [SPLIT_MAIN[-1] + N_HEADS], axis=-1)
    q = q.reshape(B, S, N_HEADS, DQK)
    k = k.reshape(B, S, N_HEADS, DQK) * (DQK ** -0.5)
    v = v.reshape(B, S, N_HEADS, DV)
    i_pre = ig + b_i.astype(jnp.float32)
    lf = jax.nn.log_sigmoid(fg + b_f.astype(jnp.float32))
    h, C, n, m = mlstm_chunked(q, k, v, i_pre, lf, C0, n0, m0)
    y = jax.nn.sigmoid(o) * head_rms_norm(h, g_head).reshape(B, S, V_WIDTH)
    return jnp.einsum('bse,ed->bsd', y.astype(x.dtype), w_out), C, n, m

def gla_mixer(x, w_in, w_gate2, b_gate, g_head, w_out, S0):
    B, S, _ = x.shape
    proj = jnp.einsum('bsd,de->bse', x, w_in).astype(jnp.float32)
    q, k, v, r, glr = jnp.split(proj, SPLIT_MAIN, axis=-1)
    q = q.reshape(B, S, N_HEADS, DQK) * (DQK ** -0.5)
    k = k.reshape(B, S, N_HEADS, DQK)
    v = v.reshape(B, S, N_HEADS, DV)
    g = jax.nn.log_sigmoid(jnp.einsum('bsr,re->bse', glr, w_gate2.astype(jnp.float32))
                           + b_gate.astype(jnp.float32)) / GATE_TAU
    g = g.reshape(B, S, N_HEADS, DQK)
    o, S_new = gla_chunked(q, k, v, g, S0)
    y = jax.nn.silu(r) * head_rms_norm(o, g_head).reshape(B, S, V_WIDTH)
    return jnp.einsum('bse,ed->bsd', y.astype(x.dtype), w_out), S_new

def swiglu(x, w_gate, w_up, w_down):
    h = jax.nn.silu(jnp.einsum('bsd,df->bsf', x, w_gate)) * jnp.einsum('bsd,df->bsf', x, w_up)
    return jnp.einsum('bsf,fd->bsd', h, w_down)

def trunk(x, C0, n0, m0, S0, w):
    (g_pre_mix, g_post_mix, g_pre_ffn, g_post_ffn,
     w_in_mlstm, b_i_mlstm, b_f_mlstm, g_head_mlstm, w_out_mlstm,
     w_in_gla, w_gate2_gla, b_gate_gla, g_head_gla, w_out_gla,
     w_ffn_gate, w_ffn_up, w_ffn_down) = w
    Cs, ns, ms, Ss = [], [], [], []
    for i in range(DEPTH):
        h = rms_norm(x, g_pre_mix[i])
        j = i // 2
        if i % 2 == 0:
            mix, C, n, m = mlstm_mixer(h, w_in_mlstm[j], b_i_mlstm[j], b_f_mlstm[j], g_head_mlstm[j],
                                       w_out_mlstm[j], C0[j], n0[j], m0[j])
            Cs.append(C); ns.append(n); ms.append(m)
        else:
            mix, S = gla_mixer(h, w_in_gla[j], w_gate2_gla[j], b_gate_gla[j], g_head_gla[j],
                               w_out_gla[j], S0[j])
            Ss.append(S)
        x = x + rms_norm(mix, g_post_mix[i])
        h = rms_norm(x, g_pre_ffn[i])
        x = x + rms_norm(swiglu(h, w_ffn_gate[i], w_ffn_up[i], w_ffn_down[i]), g_post_ffn[i])
    return x, jnp.stack(Cs), jnp.stack(ns), jnp.stack(ms), jnp.stack(Ss)

def setup_inputs(seed: int = 0) -> dict:
    key = jax.random.key(seed)
    ks = jax.random.split(key, 24)
    f32 = jnp.float32
    nrm = lambda k, shape, s: jax.random.normal(k, shape, f32) * s
    gain = lambda k, shape: 1.0 + nrm(k, shape, 0.05)
    return {
        "x_prompt": nrm(ks[0], (BATCH, SEQ, D_MODEL), 1.0),
        "x_sample": nrm(ks[1], (DEC_BATCH, DEC_SEQ, D_MODEL), 1.0),
        "state_mlstm_C": nrm(ks[2], (N_MLSTM, DEC_BATCH, N_HEADS, DQK, DV), 0.1),
        "state_mlstm_n": nrm(ks[3], (N_MLSTM, DEC_BATCH, N_HEADS, DQK), 0.5),
        "state_mlstm_m": nrm(ks[4], (N_MLSTM, DEC_BATCH, N_HEADS), 1.0),
        "state_gla_S": nrm(ks[5], (N_GLA, DEC_BATCH, N_HEADS, DQK, DV), 0.1),
        "g_pre_mix": gain(ks[6], (DEPTH, D_MODEL)),
        "g_post_mix": gain(ks[7], (DEPTH, D_MODEL)),
        "g_pre_ffn": gain(ks[8], (DEPTH, D_MODEL)),
        "g_post_ffn": gain(ks[9], (DEPTH, D_MODEL)),
        "w_in_mlstm": nrm(ks[10], (N_MLSTM, D_MODEL, MLSTM_IN), D_MODEL ** -0.5),
        "b_i_mlstm": nrm(ks[11], (N_MLSTM, N_HEADS), 0.1),
        "b_f_mlstm": FORGET_BIAS + nrm(ks[12], (N_MLSTM, N_HEADS), 0.5),
        "g_head_mlstm": gain(ks[13], (N_MLSTM, V_WIDTH)),
        "w_out_mlstm": nrm(ks[14], (N_MLSTM, V_WIDTH, D_MODEL), V_WIDTH ** -0.5),
        "w_in_gla": nrm(ks[15], (N_GLA, D_MODEL, GLA_IN), D_MODEL ** -0.5),
        "w_gate2_gla": nrm(ks[16], (N_GLA, GATE_RANK, QK_WIDTH), GATE_RANK ** -0.5),
        "b_gate_gla": nrm(ks[17], (N_GLA, QK_WIDTH), 0.1),
        "g_head_gla": gain(ks[18], (N_GLA, V_WIDTH)),
        "w_out_gla": nrm(ks[19], (N_GLA, V_WIDTH, D_MODEL), V_WIDTH ** -0.5),
        "w_ffn_gate": nrm(ks[20], (DEPTH, D_MODEL, D_FF), D_MODEL ** -0.5),
        "w_ffn_up": nrm(ks[21], (DEPTH, D_MODEL, D_FF), D_MODEL ** -0.5),
        "w_ffn_down": nrm(ks[22], (DEPTH, D_FF, D_MODEL), D_FF ** -0.5),
    }

def reference(x_prompt, x_sample, state_mlstm_C, state_mlstm_n, state_mlstm_m, state_gla_S,
              g_pre_mix, g_post_mix, g_pre_ffn, g_post_ffn,
              w_in_mlstm, b_i_mlstm, b_f_mlstm, g_head_mlstm, w_out_mlstm,
              w_in_gla, w_gate2_gla, b_gate_gla, g_head_gla, w_out_gla,
              w_ffn_gate, w_ffn_up, w_ffn_down):
    w = (g_pre_mix, g_post_mix, g_pre_ffn, g_post_ffn,
         w_in_mlstm, b_i_mlstm, b_f_mlstm, g_head_mlstm, w_out_mlstm,
         w_in_gla, w_gate2_gla, b_gate_gla, g_head_gla, w_out_gla,
         w_ffn_gate, w_ffn_up, w_ffn_down)
    Bp = x_prompt.shape[0]
    C0p = jnp.zeros((N_MLSTM, Bp, N_HEADS, DQK, DV), jnp.float32)
    n0p = jnp.zeros((N_MLSTM, Bp, N_HEADS, DQK), jnp.float32)
    m0p = jnp.zeros((N_MLSTM, Bp, N_HEADS), jnp.float32)
    S0p = jnp.zeros((N_GLA, Bp, N_HEADS, DQK, DV), jnp.float32)
    y_prompt, C_p, n_p, m_p, S_p = trunk(x_prompt, C0p, n0p, m0p, S0p, w)
    y_sample, C_s, n_s, m_s, S_s = trunk(x_sample, state_mlstm_C, state_mlstm_n, state_mlstm_m, state_gla_S, w)
    return (y_prompt, y_sample, C_p, n_p, m_p, S_p, C_s, n_s, m_s, S_s)


_drawn_inputs = setup_inputs


def setup_inputs(seed=0):
    import zlib

    import numpy as np

    out = dict(_drawn_inputs(seed))
    spreads = {}
    factors = {}
    for name, (base, spread) in spreads.items():
        noise = np.random.default_rng([zlib.crc32(name.encode()), seed]).standard_normal(out[name].shape)
        drawn = base * np.exp(spread * noise) if base else spread * noise
        out[name] = __import__('jax').numpy.asarray(drawn.astype(out[name].dtype))
    for name, factor in factors.items():
        out[name] = (out[name] * factor).astype(out[name].dtype)
    return out
```

```python
from contextlib import ExitStack

import numpy as np

import concourse.bass as bass
from concourse import mybir

F32 = mybir.dt.float32
F32R = mybir.dt.float32r
U32 = mybir.dt.uint32
ALU = mybir.AluOpType
ACT = mybir.ActivationFunctionType
AX = mybir.AxisListType

P = 128
D = 1024
KD = D // P
SEQ = 1024
NB, DS = 8, 8
TS = NB * DS
T = SEQ + TS
GRP = 3
GT = 364
TP = GRP * GT
L = 128
NC = SEQ // L
H = 4
DQK = 128
DV = 256
DFF = 2816
KF = DFF // P
EPS = 1e-6
WCOLS = 1024
QK_SCALE = float(DQK) ** -0.5
NEG = -1.0e30
ds = bass.ds

V_PRE_MIX, V_POST_MIX, V_PRE_FFN, V_POST_FFN = 0, 16, 32, 48
V_HEAD_M, V_HEAD_G, V_BGATE = 64, 72, 80
NVEC = 84


def flat(ap):
    return ap.rearrange("p g t -> p (g t)")


class Globals:
    pass


class Scope:

    def __init__(self, nc, tag):
        self.nc, self.tag, self.ctx, self.sems = nc, tag, ExitStack(), []

    def sb(self, name, shape, dt=F32):
        return self.ctx.enter_context(self.nc.sbuf_tensor(f"{self.tag}_{name}", shape, dt))

    def sem(self, name):
        self.sems.append(self.nc.alloc_semaphore(f"{self.tag}_{name}"))
        return self.sems[-1]

    def __enter__(self):
        return self

    def __exit__(self, *a):
        if self.sems and a[0] is None:
            self.nc.clear_and_free_semaphores(self.sems)
            self.nc.all_engine_barrier()
        return self.ctx.__exit__(*a)



def slot_sems(sc):
    w = Globals()
    w.landed = [sc.sem("w_landed0"), sc.sem("w_landed1")]
    w.hi, w.lo = sc.sem("w_hi_ready"), sc.sem("w_lo_ready")
    return w


def slot_load(sp, g, w, n, half, par, src, view=None):
    if not (isinstance(n, int) and n < 2):
        sp.wait_ge(w.lo, n - 1)
    dst = g.wst[:, par, :]
    if view is not None:
        dst = view(dst)
    sp.dma_start(dst, src).then_inc(w.landed[par], 16)


def slot_hi(act, g, w, half, par, units_done=None, need=None):
    act.wait_ge(w.landed[par], half * 16 + 16)
    if need is not None:
        act.wait_ge(units_done, need)
    act.activation(g.whi[:, par, :], g.wst[:, par, :], ACT.Copy).then_inc(w.hi, 1)


def slot_lo(dve, g, w, n, par):
    dve.wait_ge(w.hi, n + 1)
    dve.tensor_tensor(g.wlo[:, par, :], g.wst[:, par, :], g.whi[:, par, :].bitcast(F32),
                      ALU.subtract).then_inc(w.lo, 1)


def products(pe, g, bank0, hi, lo, par, wsl, ks, hid=None):
    mm = None
    for n, k in enumerate(ks):
        wh, wl = wsl(g.whi[:, par, :], k), wsl(g.wlo[:, par, :], k)
        for m, (wt, x) in enumerate(((wl, hi), (wh, hi), (wh, lo))):
            for t in range(GRP):
                mm = pe.matmul(g.ps[:, bank0 + t, 0:GT], wt, x[:, k, t * GT:(t + 1) * GT],
                               start=(n == 0 and m == 0), stop=(n == len(ks) - 1 and m == 2))
    return mm


def load_phase(nc, g, a):
    with Scope(nc, "in") as sc:
        xin = sc.sb("xrow", [P, 2, D])
        vrow = sc.sb("vrow", [NVEC, P])
        s_c = sc.sem("consts_landed")
        s_pad = sc.sem("pad_cleared")
        s_x = [sc.sem("x_landed0"), sc.sem("x_landed1")]
        s_t = sc.sem("x_turned")
        s_e = sc.sem("x_stored_act")
        s_f = sc.sem("x_stored_dve")
        s_v = sc.sem("vectors_turned")
        with nc.Block() as block:
            @block.sync
            def _(sp):
                for ap, src in g.const_loads:
                    sp.dma_start(ap, src).then_inc(s_c, 16)
                for r, src in ((V_PRE_MIX, a["g_pre_mix"]), (V_POST_MIX, a["g_post_mix"]),
                               (V_PRE_FFN, a["g_pre_ffn"]), (V_POST_FFN, a["g_post_ffn"]),
                               (V_HEAD_M, a["g_head_mlstm"]), (V_HEAD_G, a["g_head_gla"]),
                               (V_BGATE, a["b_gate_gla"])):
                    rows = src.rearrange("l (k p) -> (l k) p", p=P)
                    sp.dma_start(vrow[r:r + rows.shape[0], :], rows).then_inc(s_c, 16)
                for c in range(NC + 1):
                    if c >= 2:
                        sp.wait_ge(s_t, 2 * c - 2)
                    if c < NC:
                        sp.dma_start(xin[:, c % 2, :], a["x_prompt"][0, c * L:(c + 1) * L, :]
                                     ).then_inc(s_x[c % 2], 16)
                    else:
                        sp.dma_start(xin[0:TS, 0, :], a["x_sample"].rearrange("b s d -> (b s) d")
                                     ).then_inc(s_x[0], 16)

            @block.tensor
            def _(pe):
                pe.wait_ge(s_c, 16 * (len(g.const_loads) + 7))
                pe.transpose(g.ps[:, 7, 0:NVEC], vrow[:, :], g.ident[0:NVEC, 0:NVEC]).then_inc(s_v, 1)
                for c in range(NC + 1):
                    n = L if c < NC else TS
                    pe.wait_ge(s_x[c % 2], 16 * (c // 2 + 1))
                    for half, stored in ((0, s_e), (1, s_f)):
                        b = 2 * (c % 2) + half
                        if c >= 2:
                            pe.wait_ge(stored, c - 1)
                        for k in range(4):
                            mm = pe.transpose(g.ps[:, b, k * L:k * L + n],
                                              xin[0:n, c % 2, (4 * half + k) * P:(4 * half + k + 1) * P],
                                              g.ident[0:n, 0:n])
                        mm.then_inc(s_t, 1)

            def store(c, half):
                n = L if c < NC else TS
                dst = g.X[:, 4 * half:4 * half + 4, c * L:c * L + n]
                return dst, g.ps[:, 2 * (c % 2) + half, :].rearrange("p (k t) -> p k t", k=4)[:, :, 0:n]

            @block.scalar
            def _(act):
                for c in range(NC + 1):
                    act.wait_ge(s_t, 2 * c + 1)
                    act.activation(*store(c, 0), ACT.Copy).then_inc(s_e, 1)

            @block.vector
            def _(dve):
                dve.memset(g.X[:, :, T:TP], 0.0).then_inc(s_pad, 1)
                dve.wait_ge(s_v, 1)
                dve.tensor_copy(g.vec[:, :], g.ps[:, 7, 0:NVEC]).then_inc(s_pad, 1)
                for c in range(NC + 1):
                    dve.wait_ge(s_t, 2 * c + 2)
                    dve.tensor_copy(*store(c, 1)).then_inc(s_f, 1)


def by_group(ap):
    return ap.rearrange("p (g t) -> p g t", g=GRP)


def rstd_act(act, g, R, acc, s_ss, s_r):
    act.wait_ge(s_ss, 1)
    act.activation(by_group(acc[:, :]), g.ps[:, 0:GRP, 0:GT], ACT.Ln, bias=g.eps[:, 0:1]).then_inc(s_r, 1)
    act.wait_ge(s_r, 1)
    act.activation(R[:, :], acc[:, :], ACT.Exp, scale=-0.5).then_inc(s_r, 1)


def rstd_dve(dve, g, R, acc, s_r):
    dve.wait_ge(s_r, 2)
    dve.scalar_tensor_tensor(acc[:, :], R[:, :], -0.5, R[:, :], ALU.mult, ALU.mult).then_inc(s_r, 1)
    dve.wait_ge(s_r, 3)
    dve.scalar_tensor_tensor(by_group(acc[:, :]), g.ps[:, 0:GRP, 0:GT], EPS, by_group(acc[:, :]),
                             ALU.add, ALU.mult).then_inc(s_r, 1)
    dve.wait_ge(s_r, 4)
    dve.scalar_tensor_tensor(R[:, :], acc[:, :], 1.5, R[:, :], ALU.add, ALU.mult).then_inc(s_r, 1)
    dve.wait_ge(s_r, 5)


def pre_norm(nc, g, tag, col):
    with Scope(nc, tag) as sc:
        sq = sc.sb("sq", [P, 2, TP])
        acc = sc.sb("acc", [P, TP])
        R = sc.sb("rstd", [P, TP])
        t = sc.sb("t", [P, 2, TP])
        s_sq, s_acc, s_ss, s_r = (sc.sem(n) for n in ("squared", "summed", "col_sums", "rstd_steps"))
        s_t, s_hi, s_lo = (sc.sem(n) for n in ("normed", "hi_ready", "lo_ready"))
        with nc.Block() as block:
            @block.scalar
            def _(act):
                for k in range(KD):
                    if k >= 2:
                        act.wait_ge(s_acc, k - 1)
                    act.activation(sq[:, k % 2, :], g.X[:, k, :], ACT.Square).then_inc(s_sq, 1)
                rstd_act(act, g, R, acc, s_ss, s_r)
                for k in range(KD):
                    act.wait_ge(s_t, k + 1)
                    act.activation(g.HH[:, k, :], t[:, k % 2, :], ACT.Copy).then_inc(s_hi, 1)

            @block.tensor
            def _(pe):
                pe.wait_ge(s_acc, KD)
                for j in range(GRP):
                    mm = pe.matmul(g.ps[:, j, 0:GT], g.avg[:, :], acc[:, j * GT:(j + 1) * GT],
                                   start=True, stop=True)
                mm.then_inc(s_ss, 1)

            @block.vector
            def _(dve):
                for k in range(KD):
                    dve.wait_ge(s_sq, k + 1)
                    if k == 0:
                        dve.tensor_copy(acc[:, :], sq[:, 0, :]).then_inc(s_acc, 1)
                    else:
                        dve.wait_ge(s_acc, k)
                        dve.tensor_tensor(acc[:, :], acc[:, :], sq[:, k % 2, :], ALU.add).then_inc(s_acc, 1)
                rstd_dve(dve, g, R, acc, s_r)
                for k in range(KD):
                    if k >= 2:
                        dve.wait_ge(s_lo, k - 1)
                    dve.scalar_tensor_tensor(t[:, k % 2, :], g.X[:, k, :], g.vec[:, col + k:col + k + 1],
                                             R[:, :], ALU.mult, ALU.mult).then_inc(s_t, 1)

            @block.gpsimd
            def _(pool):
                for k in range(KD):
                    pool.wait_ge(s_hi, k + 1)
                    pool.tensor_tensor(g.HL[:, k, :], t[:, k % 2, :], g.HH[:, k, :].bitcast(F32),
                                       ALU.subtract).then_inc(s_lo, 1)


def post_norm(nc, g, tag, col, Y):
    with Scope(nc, tag) as sc:
        sq = sc.sb("sq", [P, 2, TP])
        acc = sc.sb("acc", [P, TP])
        R = sc.sb("rstd", [P, TP])
        s_sq, s_acc, s_ss, s_r = (sc.sem(n) for n in ("squared", "summed", "col_sums", "rstd_steps"))
        s_t, s_x = (sc.sem(n) for n in ("normed", "x_added"))
        with nc.Block() as block:
            @block.scalar
            def _(act):
                for k in range(KD):
                    if k >= 2:
                        act.wait_ge(s_acc, k - 1)
                    act.activation(sq[:, k % 2, :], Y[:, k, :], ACT.Square).then_inc(s_sq, 1)
                rstd_act(act, g, R, acc, s_ss, s_r)

            @block.tensor
            def _(pe):
                pe.wait_ge(s_acc, KD)
                for j in range(GRP):
                    mm = pe.matmul(g.ps[:, j, 0:GT], g.avg[:, :], acc[:, j * GT:(j + 1) * GT],
                                   start=True, stop=True)
                mm.then_inc(s_ss, 1)

            @block.vector
            def _(dve):
                for k in range(KD):
                    dve.wait_ge(s_sq, k + 1)
                    if k == 0:
                        dve.tensor_copy(acc[:, :], sq[:, 0, :]).then_inc(s_acc, 1)
                    else:
                        dve.wait_ge(s_acc, k)
                        dve.tensor_tensor(acc[:, :], acc[:, :], sq[:, k % 2, :], ALU.add).then_inc(s_acc, 1)
                rstd_dve(dve, g, R, acc, s_r)
                for k in range(KD):
                    dve.scalar_tensor_tensor(Y[:, k, :], Y[:, k, :], g.vec[:, col + k:col + k + 1],
                                             R[:, :], ALU.mult, ALU.mult).then_inc(s_t, 1)

            @block.gpsimd
            def _(pool):
                for k in range(KD):
                    pool.wait_ge(s_t, k + 1)
                    pool.tensor_tensor(g.X[:, k, :], g.X[:, k, :], Y[:, k, :], ALU.add).then_inc(s_x, 1)


def store_phase(nc, g, a):
    with Scope(nc, "out") as sc:
        yrow = sc.sb("yrow", [P, 2, D])
        s_t, s_e, s_f = (sc.sem(n) for n in ("y_turned", "y_copied_act", "y_copied_dve"))
        s_o = [sc.sem("y_stored0"), sc.sem("y_stored1")]
        with nc.Block() as block:
            @block.tensor
            def _(pe):
                for c in range(NC + 1):
                    n = L if c < NC else TS
                    for half, copied in ((0, s_e), (1, s_f)):
                        b = 2 * (c % 2) + half
                        if c >= 2:
                            pe.wait_ge(copied, c - 1)
                        for k in range(4):
                            mm = pe.transpose(g.ps[0:n, b, k * P:(k + 1) * P],
                                              g.X[:, 4 * half + k, c * L:c * L + n], g.ident[:, :])
                        mm.then_inc(s_t, 1)

            @block.scalar
            def _(act):
                for c in range(NC + 1):
                    n = L if c < NC else TS
                    act.wait_ge(s_t, 2 * c + 1)
                    if c >= 2:
                        act.wait_ge(s_o[c % 2], 16 * (c // 2))
                    act.activation(yrow[0:n, c % 2, 0:512], g.ps[0:n, 2 * (c % 2), :], ACT.Copy).then_inc(s_e, 1)

            @block.vector
            def _(dve):
                for c in range(NC + 1):
                    n = L if c < NC else TS
                    dve.wait_ge(s_t, 2 * c + 2)
                    if c >= 2:
                        dve.wait_ge(s_o[c % 2], 16 * (c // 2))
                    dve.tensor_copy(yrow[0:n, c % 2, 512:D], g.ps[0:n, 2 * (c % 2) + 1, :]).then_inc(s_f, 1)

            @block.sync
            def _(sp):
                for c in range(NC + 1):
                    sp.wait_ge(s_e, c + 1)
                    sp.wait_ge(s_f, c + 1)
                    if c < NC:
                        sp.dma_start(a["y_prompt"][0, c * L:(c + 1) * L, :], yrow[:, c % 2, :]
                                     ).then_inc(s_o[c % 2], 16)
                    else:
                        sp.dma_start(a["y_sample"].rearrange("b s d -> (b s) d"), yrow[0:TS, 0, :]
                                     ).then_inc(s_o[0], 16)
                sp.wait_ge(s_o[0], 16 * (NC // 2 + 1))
                sp.wait_ge(s_o[1], 16 * (NC // 2))


def ffn_phase(nc, g, tag, layer, a, Y):
    NBLK = KF // 2
    LAST = NBLK - 1
    wg = a["w_ffn_gate"][layer].rearrange("(k p) f -> p k f", p=P)
    wu = a["w_ffn_up"][layer].rearrange("(k p) f -> p k f", p=P)
    wd = a["w_ffn_down"][layer].rearrange("(k p) d -> p k d", p=P)
    cols8 = lambda w, k: w[:, k * P:(k + 1) * P]
    slot8 = lambda w: w.rearrange("p (k m) -> p k m", k=KD)
    slot2 = lambda w: w.rearrange("p (k m) -> p k m", k=2)

    with Scope(nc, tag) as sc:
        hh = sc.sb("hid_hi", [P, 2, TP], F32R)
        hl = sc.sb("hid_lo", [P, 2, TP], F32R)
        sg = sc.sb("silu", [P, 2, TP])
        pr = sc.sb("hid", [P, TP])
        w = slot_sems(sc)
        s_unit, s_silu, s_prod, s_hh, s_hl = (sc.sem(n) for n in (
            "units_done", "silu_done", "hid_done", "hid_hi_ready", "hid_lo_ready"))
        s_y = sc.sem("y_cleared_and_down_added")
        unit0 = lambda i: i * 12 + 4
        slot0 = lambda i: i * 6 + 4
        half0 = lambda i: i * 3 + 2
        banks = lambda b0: g.ps[:, b0:b0 + GRP, 0:GT]
        grp = lambda ap: ap.rearrange("p (g t) -> p g t", g=GRP)

        with nc.Block() as block:
            @block.sync
            def _(sp):
                def load(n, half, par, kind, b, c=0):
                    if kind == "down":
                        slot_load(sp, g, w, n, half, par, wd[:, ds(b * 2, 2), c * 512:(c + 1) * 512], slot2)
                    else:
                        src = wg if kind == "gate" else wu
                        slot_load(sp, g, w, n, half, par, src[:, :, ds((b * 2 + c) * P, P)], slot8)
                for n, (kind, c) in enumerate((("gate", 0), ("up", 0), ("gate", 1), ("up", 1))):
                    load(n, n // 2, n % 2, kind, 0, c)
                with sp.Fori(0, LAST) as i:
                    for j, (kind, b, c) in enumerate((("gate", i + 1, 0), ("down", i, 0), ("down", i, 1),
                                                      ("up", i + 1, 0), ("gate", i + 1, 1), ("up", i + 1, 1))):
                        load(slot0(i) + j, half0(i) + j // 2, j % 2, kind, b, c)
                for c in range(2):
                    load(slot0(LAST) + c, half0(LAST), c, "down", LAST, c)

            @block.tensor
            def _(pe):
                def tile(n, par, bank0):
                    pe.wait_ge(w.lo, n + 1)
                    products(pe, g, bank0, g.HH, g.HL, par, cols8, range(KD)).then_inc(s_unit, 1)

                def down(n, par, m0, i):
                    pe.wait_ge(w.lo, n + 1)
                    for m in range(m0, m0 + 4):
                        if m == 0:
                            pe.wait_ge(s_hl, i * 2 + 2)
                        elif m == 1:
                            pe.wait_ge(s_silu, 2 * NBLK if i is LAST else i * 2 + 3)
                        else:
                            pe.wait_ge(s_y, i * 8 + m)
                        q = m - m0
                        products(pe, g, 0 if m % 2 else 3, hh, hl, par,
                                 lambda w, k: w[:, k * 512 + q * P:k * 512 + (q + 1) * P],
                                 range(2)).then_inc(s_unit, 1)

                tile(0, 0, 0)
                tile(1, 1, 3)
                pe.wait_ge(s_silu, 1)
                tile(2, 0, 0)
                pe.wait_ge(s_prod, 1)
                tile(3, 1, 3)
                with pe.Fori(0, LAST) as i:
                    pe.wait_ge(s_silu, i * 2 + 2)
                    tile(slot0(i), 0, 0)
                    down(slot0(i) + 1, 1, 0, i)
                    down(slot0(i) + 2, 0, 4, i)
                    pe.wait_ge(s_y, i * 8 + 8)
                    tile(slot0(i) + 3, 1, 3)
                    pe.wait_ge(s_y, i * 8 + 9)
                    tile(slot0(i) + 4, 0, 0)
                    pe.wait_ge(s_prod, i * 2 + 3)
                    tile(slot0(i) + 5, 1, 3)
                down(slot0(LAST), 0, 0, LAST)
                down(slot0(LAST) + 1, 1, 4, LAST)

            @block.scalar
            def _(act):
                def silu(c, unit, before=None):
                    act.wait_ge(s_unit, unit + 1)
                    if before is not None:
                        act.wait_ge(s_prod, before)
                    act.activation(grp(sg[:, c, :]), banks(0), ACT.Silu).then_inc(s_silu, 1)

                def hid_hi(c, count, downs=None):
                    act.wait_ge(s_prod, count)
                    if downs is not None:
                        act.wait_ge(s_unit, downs)
                    act.activation(hh[:, c, :], pr[:, :], ACT.Copy).then_inc(s_hh, 1)

                slot_hi(act, g, w, 0, 0)
                slot_hi(act, g, w, 0, 1)
                silu(0, 0)
                slot_hi(act, g, w, 1, 0, s_unit, 1)
                slot_hi(act, g, w, 1, 1, s_unit, 2)
                hid_hi(0, 1)
                silu(1, 2)
                slot_hi(act, g, w, half0(0), 0, s_unit, 3)
                hid_hi(1, 2)
                with act.Fori(0, LAST) as i:
                    u = unit0(i)
                    slot_hi(act, g, w, half0(i), 1, s_unit, u)
                    silu(0, u, i * 2 + 1)
                    slot_hi(act, g, w, half0(i) + 1, 0, s_unit, u + 1)
                    slot_hi(act, g, w, half0(i) + 1, 1, s_unit, u + 5)
                    slot_hi(act, g, w, half0(i) + 2, 0, s_unit, u + 9)
                    hid_hi(0, i * 2 + 3, u + 9)
                    slot_hi(act, g, w, half0(i) + 2, 1, s_unit, u + 10)
                    silu(1, u + 10, i * 2 + 2)
                    slot_hi(act, g, w, half0(i) + 3, 0, s_unit, u + 11)
                    hid_hi(1, i * 2 + 4)
                slot_hi(act, g, w, half0(LAST), 1, s_unit, unit0(LAST))

            @block.vector
            def _(dve):
                def product(c, unit, count):
                    dve.wait_ge(s_unit, unit + 1)
                    dve.wait_ge(s_silu, count + 1)
                    if not (isinstance(count, int) and count == 0):
                        dve.wait_ge(s_hl, count)
                    dve.tensor_tensor(grp(pr[:, :]), banks(3), grp(sg[:, c, :]), ALU.mult).then_inc(s_prod, 1)
                    dve.wait_ge(s_hh, count + 1)
                    dve.tensor_tensor(hl[:, c, :], pr[:, :], hh[:, c, :].bitcast(F32),
                                      ALU.subtract).then_inc(s_hl, 1)

                def add(m, unit, count):
                    dve.wait_ge(s_unit, unit + 1)
                    dve.wait_ge(s_y, count + 1)
                    dve.tensor_tensor(grp(Y[:, m, :]), banks(0 if m % 2 else 3), grp(Y[:, m, :]),
                                      ALU.add).then_inc(s_y, 1)

                slot_lo(dve, g, w, 0, 0)
                slot_lo(dve, g, w, 1, 1)
                slot_lo(dve, g, w, 2, 0)
                slot_lo(dve, g, w, 3, 1)
                product(0, 1, 0)
                slot_lo(dve, g, w, 4, 0)
                product(1, 3, 1)
                with dve.Fori(0, LAST) as i:
                    u = unit0(i)
                    slot_lo(dve, g, w, slot0(i) + 1, 1)
                    slot_lo(dve, g, w, slot0(i) + 2, 0)
                    for m in range(4):
                        add(m, u + (1 + m), i * 8 + m)
                    slot_lo(dve, g, w, slot0(i) + 3, 1)
                    for m in range(4, 8):
                        add(m, u + (1 + m), i * 8 + m)
                    slot_lo(dve, g, w, slot0(i) + 4, 0)
                    product(0, u + 9, i * 2 + 2)
                    slot_lo(dve, g, w, slot0(i) + 5, 1)
                    slot_lo(dve, g, w, slot0(i) + 6, 0)
                    product(1, u + 11, i * 2 + 3)
                slot_lo(dve, g, w, slot0(LAST) + 1, 1)
                for m in range(8):
                    add(m, unit0(LAST) + m, LAST * 8 + m)

            @block.gpsimd
            def _(pool):
                pool.memset(Y[:, :, :], 0.0).then_inc(s_y, 1)


def wait(eng, sem, value):
    if not (isinstance(value, int) and value <= 0):
        eng.wait_ge(sem, value)


cols8 = lambda w, k: w[:, k * P:(k + 1) * P]
slot8 = lambda w: w.rearrange("p (k m) -> p k m", k=KD)


def proj_phase(nc, g, tag, a, w_in, qk_scales, gate_fn, head_col, extra_loads, GP):
    NU = 24
    wv = w_in.rearrange("(k p) e -> p k e", p=P)
    with Scope(nc, tag) as sc:
        ob = sc.sb("out", [P, 2, TP])
        w = slot_sems(sc)
        s_unit, s_copied, s_gated = (sc.sem(n) for n in ("units_done", "psum_copied", "gated"))
        s_stored = [sc.sem("stored0"), sc.sem("stored1")]
        s_z, s_e = sc.sem("extra_cleared"), sc.sem("extra_landed")
        with nc.Block() as block:
            @block.sync
            def _(sp):
                def load(n, half, par):
                    sp.wait_ge(w.lo, n + 1)
                    sp.dma_start(slot8(g.wst[:, par, :]), wv[:, :, ds(n * P, P)]).then_inc(w.landed[par], 16)

                def store(u, par, ready, count):
                    sp.wait_ge(ready, count)
                    sp.dma_start(g.PT[ds(u, 1), :, :].rearrange("m p t -> (m p) t"), ob[:, par, :]
                                 ).then_inc(s_stored[par], 16)

                for par in range(2):
                    sp.sem_inc(s_stored[par], 16)
                    load(par, 0, par)
                with sp.Fori(0, 8) as i:
                    for j in range(2):
                        load(i * 2 + (j + 2), i + 1, j)
                        store(i * 2 + j, j, s_copied, i * 2 + (j + 3))
                with sp.Fori(8, 11) as i:
                    for j in range(2):
                        load(i * 2 + (j + 2), i + 1, j)
                        store(i * 2 + j, j, s_gated, i * 2 + (j - 15))
                sp.wait_ge(s_z, 1)
                for dst, src in extra_loads:
                    sp.dma_start(dst(slot8(g.wst[:, 0, :])), src).then_inc(s_e, 16)
                for j in range(2):
                    store(22 + j, j, s_gated, 7 + j)
                for par in range(2):
                    sp.wait_ge(s_stored[par], 16 * (NU // 2 + 1))

            @block.gpsimd
            def _(pool):
                pool.wait_ge(w.lo, NU - 1 + 2)
                pool.memset(g.wst[:, 0, :], 0.0).then_inc(s_z, 1)

            @block.tensor
            def _(pe):
                pe.sem_inc(s_unit, 2)

                def unit(u, par):
                    pe.wait_ge(w.lo, u + 3)
                    pe.wait_ge(s_copied, u + 1)
                    products(pe, g, 3 * par, g.HH, g.HL, par, cols8, range(KD)).then_inc(s_unit, 1)
                with pe.Fori(0, NU // 2) as i:
                    for j in range(2):
                        unit(i * 2 + j, j)
                unit(NU, 0)

            @block.scalar
            def _(act):
                act.sem_inc(s_copied, 2)

                def hi(n, half, par):
                    act.wait_ge(w.landed[par], half * 16 + 16)
                    act.wait_ge(s_unit, n + 1)
                    act.activation(g.whi[:, par, :], g.wst[:, par, :], ACT.Copy).then_inc(w.hi, 1)

                def copy(u, half, par, func, scale=1.0):
                    act.wait_ge(s_unit, u + 3)
                    act.wait_ge(s_stored[par], half * 16 + 16)
                    act.activation(by_group(ob[:, par, :]), g.ps[:, 3 * par:3 * par + 3, 0:GT], func,
                                   scale=scale).then_inc(s_copied, 1)
                hi(0, 0, 0)
                for i0, i1, func, scale in ((0, 2, ACT.Copy, qk_scales[0]), (2, 4, ACT.Copy, qk_scales[1]),
                                            (4, 8, ACT.Copy, 1.0), (8, 11, gate_fn, 1.0)):
                    with act.Fori(i0, i1) as i:
                        hi(i * 2 + 1, i, 1)
                        copy(i * 2, i, 0, func, scale)
                        hi(i * 2 + 2, i + 1, 0)
                        copy(i * 2 + 1, i, 1, func, scale)
                hi(23, 11, 1)
                copy(22, 11, 0, gate_fn)
                act.wait_ge(s_e, 16 * len(extra_loads))
                act.wait_ge(s_unit, NU + 1)
                act.activation(g.whi[:, 0, :], g.wst[:, 0, :], ACT.Copy).then_inc(w.hi, 1)
                copy(23, 11, 1, gate_fn)
                act.wait_ge(s_unit, NU + 3)
                act.activation(by_group(GP[:, :]), g.ps[:, 0:3, 0:GT], ACT.Copy).then_inc(s_copied, 1)

            @block.vector
            def _(dve):
                dve.sem_inc(w.lo, 2)

                def lo(n, par):
                    dve.wait_ge(w.hi, n + 1)
                    dve.tensor_tensor(g.wlo[:, par, :], g.wst[:, par, :], g.whi[:, par, :].bitcast(F32),
                                      ALU.subtract).then_inc(w.lo, 1)
                lo(0, 0)
                with dve.Fori(0, 8) as i:
                    lo(i * 2 + 1, 1)
                    lo(i * 2 + 2, 0)

                def gain(u, par, col):
                    dve.wait_ge(s_copied, u + 3)
                    dve.tensor_scalar(ob[:, par, :], ob[:, par, :], g.vec[:, ds(col, 1)], None,
                                      ALU.mult).then_inc(s_gated, 1)
                with dve.Fori(0, 4) as i:
                    for j in range(2):
                        lo(i * 2 + (17 + j), 1 - j)
                        gain(i * 2 + (16 + j), j, i * 2 + (head_col + j))


def wout_phase(nc, g, tag, w_out, Y):
    wv = w_out.rearrange("(k p) e -> p k e", p=P)
    with Scope(nc, tag) as sc:
        w = slot_sems(sc)
        s_unit, s_copied = sc.sem("units_done"), sc.sem("psum_copied")
        with nc.Block() as block:
            @block.sync
            def _(sp):
                with sp.Fori(0, KD // 2) as i:
                    for par in range(2):
                        sp.wait_ge(w.lo, i * 2 + (par + 1))
                        sp.dma_start(slot8(g.wst[:, par, :]), wv[:, :, ds((i * 2 + par) * P, P)]
                                     ).then_inc(w.landed[par], 16)

            @block.tensor
            def _(pe):
                pe.sem_inc(s_unit, 2)
                with pe.Fori(0, KD // 2) as i:
                    for par in range(2):
                        pe.wait_ge(w.lo, i * 2 + (par + 3))
                        pe.wait_ge(s_copied, i * 2 + (par + 1))
                        products(pe, g, 3 * par, g.HH, g.HL, par, cols8, range(KD)).then_inc(s_unit, 1)

            @block.scalar
            def _(act):
                act.sem_inc(s_copied, 2)

                def hi(n, half, par):
                    act.wait_ge(w.landed[par], half * 16 + 16)
                    act.wait_ge(s_unit, n + 1)
                    act.activation(g.whi[:, par, :], g.wst[:, par, :], ACT.Copy).then_inc(w.hi, 1)

                def copy(u, par):
                    act.wait_ge(s_unit, u + 3)
                    act.activation(by_group(Y[:, ds(u, 1), :].rearrange("p m t -> p (m t)")),
                                   g.ps[:, 3 * par:3 * par + 3, 0:GT], ACT.Copy).then_inc(s_copied, 1)
                hi(0, 0, 0)
                with act.Fori(0, KD // 2 - 1) as i:
                    hi(i * 2 + 1, i, 1)
                    copy(i * 2, 0)
                    hi(i * 2 + 2, i + 1, 0)
                    copy(i * 2 + 1, 1)
                hi(KD - 1, KD // 2 - 1, 1)
                copy(KD - 2, 0)
                copy(KD - 1, 1)

            @block.vector
            def _(dve):
                dve.sem_inc(w.lo, 2)
                with dve.Fori(0, KD // 2) as i:
                    for par in range(2):
                        dve.wait_ge(w.hi, i * 2 + (par + 1))
                        dve.tensor_tensor(g.wlo[:, par, :], g.wst[:, par, :], g.whi[:, par, :].bitcast(F32),
                                          ALU.subtract).then_inc(w.lo, 1)


def chunk_io(c):
    return c * L, (TS if isinstance(c, int) and c == NC else L)


def cheads(ap):
    return ap.rearrange("p (h t) -> p h t", h=H)


def gates_mlstm(nc, g, tag, a, GP, m):
    with Scope(nc, tag) as sc:
        Z = sc.sb("z", [H, TP])
        I = sc.sb("i", [H, TP])
        T1 = sc.sb("t1", [H, TP])
        LF = sc.sb("lf", [H, TP])
        B = sc.sb("b", [H, TP])
        M = sc.sb("m", [H, TP])
        W = sc.sb("wrow", [H, TP])
        EM = sc.sb("negm", [H, TP])
        WS = sc.sb("wsrow", [H, TP])
        MP = sc.sb("m_before", [H, NC + NB])
        DL = sc.sb("declog", [H, NC + NB])
        DD = sc.sb("decdiag", [H, NC + NB, H])
        bi = sc.sb("bi", [H, 2])
        s_in, s_d, s_a, s_p, s_out = (sc.sem(n) for n in (
            "small_landed", "dve_steps", "act_steps", "turned", "m_stored"))
        steps = {"n": 0}

        def nat(n, c0, c1, q0, q1):
            return g.ps[0:n, 0, 0:(NC + 1) * 3 * H].rearrange("p (c q) -> p c q", c=NC + 1)[:, c0:c1, q0:q1]

        with nc.Block() as block:
            @block.sync
            def _(sp):
                sp.dma_start(bi[:, 0:1], a["b_i_mlstm"].rearrange("l h -> h l")).then_inc(s_in, 16)
                sp.dma_start(bi[:, 1:2], a["b_f_mlstm"].rearrange("l h -> h l")).then_inc(s_in, 16)
                sp.dma_start(MP[:, NC:NC + NB], a["state_mlstm_m"].rearrange("l b h -> (l h) b"),
                             allow_slow_non_contiguous=True).then_inc(s_in, 16)
                sp.wait_ge(s_d, 11)
                sp.dma_start(a["m_prompt"].rearrange("l b h -> (l h) b"), M[:, SEQ - 1:SEQ],
                             allow_slow_non_contiguous=True).then_inc(s_out, 16)
                sp.dma_start(a["m_sample"].rearrange("l b h -> (l h) b"), M[:, SEQ + DS - 1:T:DS],
                             allow_slow_non_contiguous=True).then_inc(s_out, 16)
                sp.wait_ge(s_out, 32)

            @block.vector
            def _(dve):
                def step(ins):
                    steps["n"] += 1
                    ins.then_inc(s_d, 1)
                    dve.wait_ge(s_d, steps["n"])
                dve.wait_ge(s_in, 48)
                step(dve.tensor_scalar(I[:, :], GP[0:H, :], bi[:, 0:1], None, ALU.add))
                step(dve.tensor_copy(Z[:, :], GP[32:32 + H, :]))
                step(dve.tensor_scalar(Z[:, :], Z[:, :], bi[:, 1:2], None, ALU.add))
                dve.wait_ge(s_a, 3)
                step(dve.scalar_tensor_tensor(LF[:, :], Z[:, :], 0.0, T1[:, :], ALU.min, ALU.subtract))
                step(dve.tensor_tensor_scan(B[:, :], g.reset[0:H, :], LF[:, :], 0.0, ALU.mult, ALU.add))
                dve.tensor_tensor_scan(M[:, 0:SEQ], LF[:, 0:SEQ], I[:, 0:SEQ], 0.0, ALU.add, ALU.max)
                for b in range(NB):
                    t0 = SEQ + b * DS
                    ins = dve.tensor_tensor_scan(M[:, t0:t0 + DS], LF[:, t0:t0 + DS], I[:, t0:t0 + DS],
                                                 MP[:, NC + b:NC + b + 1], ALU.add, ALU.max)
                step(ins)
                step(dve.memset(M[:, T:TP], 0.0))
                step(dve.memset(MP[:, 0:1], 0.0))
                step(dve.tensor_copy(MP[:, 1:NC], M[:, L - 1:SEQ - 1:L]))
                step(dve.tensor_tensor(m.U[:, :], B[:, :], M[:, :], ALU.subtract))
                step(dve.tensor_tensor(W[:, :], I[:, :], B[:, :], ALU.subtract))
                step(dve.tensor_tensor(m.WI[:, 0:SEQ].rearrange("p (c t) -> p c t", t=L),
                                       m.U[:, 0:SEQ].rearrange("p (c t) -> p c t", t=L),
                                       MP[:, 0:NC].unsqueeze(2).to_broadcast([H, NC, L]), ALU.add))
                step(dve.tensor_tensor(m.WI[:, SEQ:T].rearrange("p (c t) -> p c t", t=DS),
                                       m.U[:, SEQ:T].rearrange("p (c t) -> p c t", t=DS),
                                       MP[:, NC:NC + NB].unsqueeze(2).to_broadcast([H, NB, DS]), ALU.add))
                step(dve.tensor_tensor(WS[:, 0:SEQ].rearrange("p (c t) -> p c t", t=L),
                                       W[:, 0:SEQ].rearrange("p (c t) -> p c t", t=L),
                                       m.U[:, L - 1:SEQ:L].unsqueeze(2).to_broadcast([H, NC, L]), ALU.add))
                step(dve.tensor_tensor(WS[:, SEQ:T].rearrange("p (c t) -> p c t", t=DS),
                                       W[:, SEQ:T].rearrange("p (c t) -> p c t", t=DS),
                                       m.U[:, SEQ + DS - 1:T:DS].unsqueeze(2).to_broadcast([H, NB, DS]), ALU.add))
                step(dve.tensor_tensor(DL[:, 0:NC], m.U[:, L - 1:SEQ:L], MP[:, 0:NC], ALU.add))
                step(dve.tensor_tensor(DL[:, NC:NC + NB], m.U[:, SEQ + DS - 1:T:DS], MP[:, NC:NC + NB], ALU.add))
                step(dve.tensor_tensor(DD[:, :, :], DL[:, :].unsqueeze(2).to_broadcast([H, NC + NB, H]),
                                       g.ident[0:H, 0:H].unsqueeze(1).to_broadcast([H, NC + NB, H]), ALU.mult))
                dve.wait_ge(s_p, 1)
                dve.tensor_copy(m.NAT[:, 0:NC, 0:H], nat(P, 0, NC, 0, H))
                step(dve.tensor_copy(m.NAT[0:TS, NC:NC + 1, 0:H], nat(TS, NC, NC + 1, 0, H)))

            @block.scalar
            def _(act):
                act.wait_ge(s_d, 3)
                act.activation(T1[:, :], Z[:, :], ACT.Abs).then_inc(s_a, 1)
                act.wait_ge(s_a, 1)
                act.activation(T1[:, :], T1[:, :], ACT.Exp, scale=-1.0).then_inc(s_a, 1)
                act.wait_ge(s_a, 2)
                act.activation(T1[:, :], T1[:, :], ACT.Ln, bias=1.0).then_inc(s_a, 1)
                act.wait_ge(s_d, 13)
                act.activation(m.WI[:, 0:T], m.WI[:, 0:T], ACT.Exp).then_inc(s_a, 1)
                act.wait_ge(s_p, 1)
                act.wait_ge(s_d, 19)
                act.activation(m.NAT[:, 0:NC, H:3 * H], nat(P, 0, NC, H, 3 * H), ACT.Exp)
                act.activation(m.NAT[0:TS, NC:NC + 1, H:3 * H], nat(TS, NC, NC + 1, H, 3 * H), ACT.Exp).then_inc(s_a, 1)
                act.activation(m.DEC[:, :, :], g.ps[:, 1, 0:(NC + NB) * H].rearrange(
                    "p (c h) -> p c h", h=H), ACT.Exp).then_inc(s_a, 1)

            @block.tensor
            def _(pe):
                pe.wait_ge(s_d, 18)
                for c in range(NC + 1):
                    n = L if c < NC else TS
                    for q, row in enumerate((W, EM, WS)):
                        scale = g.negi[:, :] if row is EM else g.ident[0:H, 0:H]
                        src = M if row is EM else row
                        pe.matmul(g.ps[0:n, 0, (c * 3 + q) * H:(c * 3 + q + 1) * H],
                                  src[:, c * L:c * L + n], scale, start=True, stop=True)
                pe.matmul(g.ps[:, 1, 0:(NC + NB) * H], g.ones[0:H, :],
                          DD[:, :, :].rearrange("p c h -> p (c h)"), start=True, stop=True).then_inc(s_p, 1)


def mlstm_mix(nc, g, tag, a, m):
    with Scope(nc, tag) as sc:
        inp = sc.sb("qkvo", [P, 2, 24, L])
        VA = sc.sb("v_one", [P, H, DV + 1])
        KW = sc.sb("k_weighted", [P, H, DQK])
        QW = sc.sb("q_weighted", [P, H, L])
        E = sc.sb("decays", [P, H, L])
        A = sc.sb("scores", [P, H, L])
        YN = sc.sb("y_normed", [P, H, DV])
        TT = sc.sb("y_gated", [P, KD, L])
        C = sc.sb("state", [P, H, DV + 1])
        SM = sc.sb("small", [P, 8, H])
        mask = sc.sb("mask", [P, L])
        mask8 = sc.sb("mask8", [TS, TS])
        CS = sc.sb("sample_state", [P, 2, H, DV + 1])
        KB = g.wst[0:TS, 0, :].rearrange("p (b h d) -> p b h d", b=2, h=H)
        QB = g.wst[:, 1, 0:2 * H * TS].rearrange("p (b h t) -> p b h t", b=2, h=H)
        bm = g.wst[:, 1, 2 * H * TS:].rearrange("p (b t) -> p b t", b=NB)
        bmr = sc.sb("batch_rows", [TS, NB])
        names = ("consts", "k_turned", "v_turned", "s_ready", "u_ready", "wi_ready", "k_scaled", "v_copied",
                 "masked", "decays_ready", "scores_ready", "q_scaled", "num_ready", "sq_ready", "ln_ready",
                 "yn_ready", "state_ready", "state_added", "y_turned", "y_gated", "hi_ready", "lo_ready",
                 "small_steps", "newton_done", "scale_ready", "ones_ready", "stored", "est_ready", "qb_ready", "kb_ready", "b_inter", "b_state",
                 "b_added")
        s = {name: sc.sem(name) for name in names}
        landed = [sc.sem("landed0"), sc.sem("landed1")]
        c_landed = [sc.sem("c_landed0"), sc.sem("c_landed1")]
        c_stored = [sc.sem("c_stored0"), sc.sem("c_stored1")]
        ps = g.ps
        bank = lambda b, n=L: ps[:, b, :].rearrange("p (h t) -> p h t", h=H)[:, :, 0:n]

        def tokens(c):
            return ds(c * L, TS if isinstance(c, int) and c == NC else L)

        C_in = a["state_mlstm_C"].rearrange("l b h d v -> (l b) d h v")
        n_in = a["state_mlstm_n"].rearrange("l b h d -> (l b) d h")
        C_out = a["C_sample"].rearrange("l b h d v -> (l b) d h v")
        n_out = a["n_sample"].rearrange("l b h d -> (l b) d h")
        with nc.Block() as block:
            def store_state(sp, b):
                par = b % 2
                sp.wait_ge(s["b_added"], b + 1)
                sp.dma_start(C_out[b], CS[:, par, :, 0:DV]).then_inc(c_stored[par], 16)
                sp.dma_start(n_out[b].unsqueeze(2), CS[:, par, :, DV:DV + 1],
                             allow_slow_non_contiguous=True).then_inc(c_stored[par], 16)

            @block.sync
            def _(sp):
                sp.dma_start(mask[:, :], a["c_causal"]).then_inc(s["consts"], 16)
                sp.dma_start(mask8[:, :], a["c_causal8"]).then_inc(s["consts"], 16)
                sp.dma_start(bm[:, :, :], a["c_batch_cols"]).then_inc(s["consts"], 16)
                sp.dma_start(bmr[:, :], a["c_batch_rows"]).then_inc(s["consts"], 16)

                def load(c, half, par):
                    n = TS if isinstance(c, int) and c == NC else L
                    wait(sp, s["y_gated"], c - 1)
                    sp.dma_start(inp[:, par, :, 0:n], g.PT[0:24, :, ds(c * L, n)].rearrange("m p t -> p m t")
                                 ).then_inc(landed[par], 16)
                load(0, 0, 0)
                load(1, 0, 1)
                with sp.Fori(1, NC // 2) as i:
                    for par in range(2):
                        load(i * 2 + par, i, par)
                load(NC, NC // 2, 0)
                sp.wait_ge(s["state_added"], NC + 1)
                sp.dma_start(a["C_prompt"].rearrange("l b h d v -> (l b d) h v"), C[:, :, 0:DV]).then_inc(s["stored"], 16)
                sp.dma_start(a["n_prompt"].rearrange("l b h d -> (l b d) h").unsqueeze(2), C[:, :, DV:DV + 1],
                             allow_slow_non_contiguous=True).then_inc(s["stored"], 16)
                for b in range(NB):
                    par = b % 2
                    if b >= 2:
                        sp.wait_ge(c_stored[par], 32 * (b // 2))
                    sp.dma_start(CS[:, par, :, 0:DV], C_in[b]).then_inc(c_landed[par], 16)
                    sp.dma_start(CS[:, par, :, DV:DV + 1], n_in[b].unsqueeze(2),
                                 allow_slow_non_contiguous=True).then_inc(c_landed[par], 16)
                    if b >= 1:
                        store_state(sp, b - 1)
                store_state(sp, NB - 1)
                sp.wait_ge(s["stored"], 32)
                for par in range(2):
                    sp.wait_ge(c_stored[par], 32 * (NB // 2))

            @block.tensor
            def _(pe):
                def scores(c, half, par):
                    sample = isinstance(c, int) and c == NC
                    n = TS if sample else L
                    x = inp[:, par, :, :]
                    pe.wait_ge(landed[par], half * 16 + 16)
                    pe.wait_ge(s["state_added"], c + 1)
                    for h in range(H):
                        mm = pe.transpose(ps[0:n, 0, h * L:(h + 1) * L], x[:, 4 + h, 0:n], g.ident[:, :])
                    mm.then_inc(s["k_turned"], 1)
                    for j in range(8):
                        mm = pe.transpose(ps[0:n, 1 + j // 4, (j % 4) * P:(j % 4 + 1) * P], x[:, 8 + j, 0:n],
                                          g.ident[:, :])
                    mm.then_inc(s["v_turned"], 1)
                    for h in range(H):
                        mm = pe.matmul(ps[0:n, 3, h * L:h * L + n], x[:, 4 + h, 0:n], x[:, h, 0:n],
                                       start=True, stop=True)
                    mm.then_inc(s["s_ready"], 1)
                    wait(pe, s["y_gated"], c)
                    for h in range(H):
                        mm = pe.matmul(ps[:, 4, h * L:h * L + n], g.sel[:, h, :], m.U[:, ds(c * L, n)],
                                       start=True, stop=True)
                    mm.then_inc(s["u_ready"], 1)
                    for h in range(H):
                        mm = pe.matmul(ps[:, 5, h * L:h * L + n], g.sel[:, h, :], m.WI[:, ds(c * L, n)],
                                       start=True, stop=True)
                    mm.then_inc(s["wi_ready"], 1)

                def turn_y(c):
                    n = TS if isinstance(c, int) and c == NC else L
                    pe.wait_ge(s["yn_ready"], c + 1)
                    for j in range(8):
                        mm = pe.transpose(ps[:, 4 + j // 4, (j % 4) * L:(j % 4) * L + n],
                                          YN[0:n, j // 2, (j % 2) * P:(j % 2 + 1) * P], g.ident[0:n, 0:n])
                    mm.then_inc(s["y_turned"], 1)

                def chunk(c, half, par):
                    scores(c, half, par)
                    pe.wait_ge(s["q_scaled"], c + 1)
                    pe.wait_ge(s["masked"], c + 1)
                    pe.wait_ge(s["scores_ready"], c + 1)
                    pe.wait_ge(s["v_copied"], c + 1)
                    for h in range(H):
                        pe.matmul(ps[:, 4 + h, 0:DV + 1], QW[:, h, :], C[:, h, :], start=True, stop=False)
                        mm = pe.matmul(ps[:, 4 + h, 0:DV + 1], A[:, h, :], VA[:, h, :], start=False, stop=True)
                    mm.then_inc(s["num_ready"], 1)
                    pe.wait_ge(s["k_scaled"], c + 1)
                    for h in range(H):
                        mm = pe.matmul(ps[:, h, 0:DV + 1], KW[:, h, :], VA[:, h, :], start=True, stop=True)
                    mm.then_inc(s["state_ready"], 1)
                    turn_y(c)

                pe.wait_ge(s["ones_ready"], 1)
                chunk(0, 0, 0)
                chunk(1, 0, 1)
                with pe.Fori(1, NC // 2) as i:
                    for par in range(2):
                        chunk(i * 2 + par, i, par)
                scores(NC, NC // 2, 0)
                pe.wait_ge(s["q_scaled"], NC + 1)
                pe.wait_ge(s["masked"], NC + 1)
                pe.wait_ge(s["scores_ready"], NC + 1)
                pe.wait_ge(s["v_copied"], NC + 1)
                pe.wait_ge(s["k_scaled"], NC + 1)
                for h in range(H):
                    pe.matmul(ps[0:TS, 4 + h, 0:DV + 1], A[0:TS, h, 0:TS], VA[0:TS, h, :], start=True, stop=False)
                for b in range(NB):
                    pe.wait_ge(c_landed[b % 2], 32 * (b // 2 + 1))
                    pe.wait_ge(s["qb_ready"], b + 1)
                    for h in range(H):
                        mm = pe.matmul(ps[0:TS, 4 + h, 0:DV + 1], QB[:, b % 2, h, :], CS[:, b % 2, h, :],
                                       start=False, stop=(b == NB - 1))
                    mm.then_inc(s["b_inter"], 1)
                    pe.wait_ge(s["kb_ready"], b + 1)
                    wait(pe, s["b_added"], b)
                    for h in range(H):
                        mm = pe.matmul(ps[:, h, 0:DV + 1], KB[:, b % 2, h, :], VA[0:TS, h, :], start=True, stop=True)
                    mm.then_inc(s["b_state"], 1)
                turn_y(NC)

            @block.scalar
            def _(act):
                def first(c):
                    n = TS if isinstance(c, int) and c == NC else L
                    act.wait_ge(s["k_turned"], c + 1)
                    wait(act, s["state_ready"], c)
                    for h in range(H):
                        ins = act.activation(KW[0:n, h, :], bank(0)[0:n, h, :], ACT.Copy,
                                             scale=m.NAT[0:n, ds(c, 1), 2 * H + h:2 * H + h + 1].rearrange("p a b -> p (a b)"))
                    ins.then_inc(s["k_scaled"], 1)
                    act.wait_ge(s["v_turned"], c + 1)
                    act.activation(VA[0:n, :, 0:DV], ps[0:n, 1:3, :].rearrange("p b (h v) -> p (b h) v", h=2),
                                   ACT.Copy).then_inc(s["v_copied"], 1)
                    act.wait_ge(s["masked"], c + 1)
                    for h in range(H):
                        ins = act.activation(E[0:n, h, 0:n], E[0:n, h, 0:n], ACT.Exp,
                                             bias=m.NAT[0:n, ds(c, 1), h:h + 1].rearrange("p a b -> p (a b)"))
                    ins.then_inc(s["decays_ready"], 1)

                def second(c):
                    n = TS if isinstance(c, int) and c == NC else L
                    act.wait_ge(s["small_steps"], c * 7 + 4)
                    for h in range(H):
                        ins = act.activation(YN[0:n, h, :], ps[0:n, 4 + h, 0:DV], ACT.Square,
                                             scale=SM[0:n, 2, h:h + 1], accum_out=SM[0:n, 3, h:h + 1])
                    ins.then_inc(s["sq_ready"], 1)
                    act.wait_ge(s["sq_ready"], c + 1)
                    act.activation(SM[0:n, 4, :], SM[0:n, 3, :], ACT.Ln, bias=g.eps[0:n, 0:1], scale=1.0 / DV
                                   ).then_inc(s["ln_ready"], 1)
                    act.wait_ge(s["ln_ready"], c + 1)
                    act.activation(SM[0:n, 5, :], SM[0:n, 4, :], ACT.Exp, scale=-0.5).then_inc(s["est_ready"], 1)
                    act.wait_ge(s["y_gated"], c + 1)
                    act.activation(g.HH[:, :, ds(c * L, n)], TT[:, :, 0:n], ACT.Copy).then_inc(s["hi_ready"], 1)

                def both(c):
                    first(c)
                    second(c)
                both(0)
                both(1)
                with act.Fori(1, NC // 2) as i:
                    for par in range(2):
                        both(i * 2 + par)
                both(NC)

            @block.vector
            def _(dve):
                def first(c, half, par):
                    sample = isinstance(c, int) and c == NC
                    n = TS if sample else L
                    mk = mask8 if sample else mask
                    dve.wait_ge(s["u_ready"], c + 1)
                    wait(dve, s["scores_ready"], c)
                    dve.tensor_tensor(E[0:n, :, 0:n], bank(4, n)[0:n], mk[:, :].unsqueeze(1).to_broadcast([n, H, n]),
                                      ALU.add).then_inc(s["masked"], 1)
                    dve.wait_ge(s["wi_ready"], c + 1)
                    wait(dve, s["num_ready"], c)
                    dve.tensor_tensor(QW[:, :, 0:n], inp[:, par, 0:H, 0:n], bank(5, n), ALU.mult).then_inc(s["q_scaled"], 1)
                    dve.wait_ge(s["s_ready"], c + 1)
                    dve.wait_ge(s["decays_ready"], c + 1)
                    dve.tensor_tensor(A[0:n, :, 0:n], bank(3, n)[0:n], E[0:n, :, 0:n], ALU.mult).then_inc(s["scores_ready"], 1)

                def second(c, par):
                    n = TS if isinstance(c, int) and c == NC else L
                    base = c * 7
                    if not (isinstance(c, int) and c == NC):
                        dve.wait_ge(s["num_ready"], c + 1)
                    den = ps[0:n, 4:8, DV:DV + 1].rearrange("p h o -> p (h o)")
                    dve.tensor_copy(SM[0:n, 0, :], den).then_inc(s["small_steps"], 1)
                    dve.wait_ge(s["small_steps"], base + 1)
                    dve.scalar_tensor_tensor(SM[0:n, 1, :], SM[0:n, 0, :], -1.0, SM[0:n, 0, :], ALU.mult, ALU.max
                                             ).then_inc(s["small_steps"], 1)
                    dve.wait_ge(s["small_steps"], base + 2)
                    dve.tensor_tensor(SM[0:n, 1, :], SM[0:n, 1, :],
                                      m.NAT[0:n, ds(c, 1), H:2 * H].rearrange("p a b -> p (a b)"), ALU.max
                                      ).then_inc(s["small_steps"], 1)
                    dve.wait_ge(s["small_steps"], base + 3)
                    dve.reciprocal(SM[0:n, 2, :], SM[0:n, 1, :]).then_inc(s["small_steps"], 1)
                    dve.wait_ge(s["est_ready"], c + 1)
                    dve.tensor_scalar(SM[0:n, 3, :], SM[0:n, 3, :], 1.0 / DV, EPS, ALU.mult, ALU.add
                                      ).then_inc(s["small_steps"], 1)
                    dve.scalar_tensor_tensor(SM[0:n, 6, :], SM[0:n, 5, :], -0.5, SM[0:n, 5, :], ALU.mult, ALU.mult
                                             ).then_inc(s["small_steps"], 1)
                    dve.wait_ge(s["small_steps"], base + 6)
                    dve.tensor_tensor(SM[0:n, 6, :], SM[0:n, 6, :], SM[0:n, 3, :], ALU.mult).then_inc(s["small_steps"], 1)
                    dve.wait_ge(s["small_steps"], base + 7)
                    dve.scalar_tensor_tensor(SM[0:n, 6, :], SM[0:n, 6, :], 1.5, SM[0:n, 5, :], ALU.add, ALU.mult
                                             ).then_inc(s["newton_done"], 1)
                    dve.wait_ge(s["newton_done"], c + 1)
                    dve.tensor_tensor(SM[0:n, 7, :], SM[0:n, 6, :], SM[0:n, 2, :], ALU.mult).then_inc(s["scale_ready"], 1)
                    dve.wait_ge(s["scale_ready"], c + 1)
                    for h in range(H):
                        ins = dve.tensor_scalar(YN[0:n, h, :], ps[0:n, 4 + h, 0:DV], SM[0:n, 7, h:h + 1], None, ALU.mult)
                    ins.then_inc(s["yn_ready"], 1)

                def state(c):
                    dve.wait_ge(s["state_ready"], c + 1)
                    for h in range(H):
                        ins = dve.scalar_tensor_tensor(
                            C[:, h, :], C[:, h, :], m.DEC[:, ds(c, 1), h:h + 1].rearrange("p a b -> p (a b)"),
                            ps[:, h, 0:DV + 1], ALU.mult, ALU.add)
                    ins.then_inc(s["state_added"], 1)

                def gated(c, par):
                    n = TS if isinstance(c, int) and c == NC else L
                    dve.wait_ge(s["y_turned"], c + 1)
                    wait(dve, s["lo_ready"], c)
                    dve.tensor_tensor(TT[:, :, 0:n], ps[:, 4:6, :].rearrange("p b (j t) -> p (b j) t", j=4)[:, :, 0:n],
                                      inp[:, par, 16:24, 0:n], ALU.mult).then_inc(s["y_gated"], 1)

                def chunk(c, half, par):
                    first(c, half, par)
                    second(c, par)
                    state(c)
                    gated(c, par)

                dve.memset(C[:, :, :], 0.0).then_inc(s["state_added"], 1)
                dve.memset(VA[:, :, DV:DV + 1], 1.0).then_inc(s["ones_ready"], 1)
                dve.wait_ge(s["consts"], 64)
                chunk(0, 0, 0)
                chunk(1, 0, 1)
                with dve.Fori(1, NC // 2) as i:
                    for par in range(2):
                        chunk(i * 2 + par, i, par)
                first(NC, NC // 2, 0)
                for b in range(NB):
                    wait(dve, s["b_inter"], b - 1)
                    dve.wait_ge(s["q_scaled"], NC + 1)
                    dve.tensor_tensor(QB[:, b % 2, :, :], QW[:, :, 0:TS],
                                      bm[:, b, :].unsqueeze(1).to_broadcast([P, H, TS]), ALU.mult).then_inc(s["qb_ready"], 1)
                    wait(dve, s["b_state"], b - 1)
                    dve.wait_ge(s["k_scaled"], NC + 1)
                    dve.tensor_scalar(KB[:, b % 2, :, :], KW[0:TS, :, :], bmr[:, b:b + 1], None, ALU.mult
                                      ).then_inc(s["kb_ready"], 1)
                    dve.wait_ge(s["b_state"], b + 1)
                    dve.wait_ge(s["b_inter"], b + 1)
                    for h in range(H):
                        ins = dve.scalar_tensor_tensor(CS[:, b % 2, h, :], CS[:, b % 2, h, :],
                                                       m.DEC[:, NC + b, h:h + 1], ps[:, h, 0:DV + 1], ALU.mult, ALU.add)
                    ins.then_inc(s["b_added"], 1)
                second(NC, 0)
                gated(NC, 0)

            @block.gpsimd
            def _(pool):
                def low(c):
                    n = TS if isinstance(c, int) and c == NC else L
                    pool.wait_ge(s["hi_ready"], c + 1)
                    pool.tensor_tensor(g.HL[:, :, ds(c * L, n)], TT[:, :, 0:n],
                                       g.HH[:, :, ds(c * L, n)].bitcast(F32), ALU.subtract).then_inc(s["lo_ready"], 1)
                low(0)
                low(1)
                with pool.Fori(1, NC // 2) as i:
                    for par in range(2):
                        low(i * 2 + par)
                low(NC)


def gates_gla(nc, g, tag, a, GP):
    with Scope(nc, tag) as sc:
        W2 = sc.sb("w_gate2", [16, H * DQK])
        T1 = sc.sb("softplus", [P, TP])
        ZM = sc.sb("z_min", [P, TP])
        B = sc.sb("b", [P, 2, TP])
        s_in, s_z, s_a, s_m, s_d, s_b = (sc.sem(n) for n in (
            "w_landed", "z_ready", "act_steps", "z_min_ready", "log_ready", "summed"))
        s_out = [sc.sem("stored0"), sc.sem("stored1")]
        with nc.Block() as block:
            @block.sync
            def _(sp):
                sp.dma_start(W2[:, :], a["w_gate2_gla"][0]).then_inc(s_in, 16)
                for h in range(H):
                    sp.wait_ge(s_b, h + 1)
                    sp.dma_start(g.PT[24 + h, :, :], B[:, h % 2, :]).then_inc(s_out[h % 2], 16)
                for par in range(2):
                    sp.wait_ge(s_out[par], 32)

            @block.tensor
            def _(pe):
                pe.wait_ge(s_in, 16)
                for h in range(H):
                    b0 = 3 * (h % 2)
                    if h >= 2:
                        pe.wait_ge(s_a, 3 * (h - 2) + 1)
                        pe.wait_ge(s_m, h - 1)
                    for t in range(GRP):
                        mm = pe.matmul(g.ps[:, b0 + t, 0:GT], W2[:, h * DQK:(h + 1) * DQK],
                                       GP[0:16, t * GT:(t + 1) * GT], start=True, stop=True)
                    mm.then_inc(s_z, 1)

            @block.scalar
            def _(act):
                for h in range(H):
                    b0 = 3 * (h % 2)
                    act.wait_ge(s_m, h + 1)
                    wait(act, s_d, h)
                    act.activation(by_group(T1[:, :]), g.ps[:, b0:b0 + 3, 0:GT], ACT.Abs,
                                   bias=g.vec[:, V_BGATE + h:V_BGATE + h + 1]).then_inc(s_a, 1)
                    act.wait_ge(s_a, 3 * h + 1)
                    act.activation(T1[:, :], T1[:, :], ACT.Exp, scale=-1.0).then_inc(s_a, 1)
                    act.wait_ge(s_a, 3 * h + 2)
                    act.activation(T1[:, :], T1[:, :], ACT.Ln, bias=1.0).then_inc(s_a, 1)

            @block.vector
            def _(dve):
                for h in range(H):
                    b0 = 3 * (h % 2)
                    dve.wait_ge(s_z, h + 1)
                    wait(dve, s_b, h)
                    dve.tensor_scalar(by_group(ZM[:, :]), g.ps[:, b0:b0 + 3, 0:GT],
                                      g.vec[:, V_BGATE + h:V_BGATE + h + 1], 0.0, ALU.add, ALU.min).then_inc(s_m, 1)
                    dve.wait_ge(s_a, 3 * h + 3)
                    dve.wait_ge(s_m, h + 1)
                    dve.tensor_tensor(ZM[:, :], ZM[:, :], T1[:, :], ALU.subtract).then_inc(s_d, 1)
                    dve.wait_ge(s_d, h + 1)
                    if h >= 2:
                        dve.wait_ge(s_out[h % 2], 16)
                    dve.tensor_tensor_scan(B[:, h % 2, :], g.reset[:, :], ZM[:, :], 0.0, ALU.mult, ALU.add
                                           ).then_inc(s_b, 1)


LEVELS = (64, 32, 16, 8, 4, 2, 1)
ITAU = 1.0 / 16.0


def gla_mix(nc, g, tag, a):
    NLV = len(LEVELS)
    with Scope(nc, tag) as sc:
        inp = sc.sb("qkvrb", [P, 2, 28, L])
        XL = sc.sb("levels", [P, NLV, H, L])
        EB = sc.sb("exp_b", [P, H, L])
        KD = sc.sb("k_decayed", [P, H, L])
        QE = sc.sb("q_decayed", [P, H, L])
        VN = sc.sb("v", [P, H, DV])
        S = sc.sb("state", [P, H, DV])
        YN = sc.sb("y_normed", [P, H, DV])
        TT = sc.sb("y_gated", [P, D // P, L])
        SM = sc.sb("small", [P, 8, H])
        masks = sc.sb("masks", [P, NLV + 1, L], U32)
        bmr = sc.sb("batch_rows", [TS, NB])
        A = cheads(g.wst[:, 0, 0:512])
        KN = cheads(g.wst[:, 0, 512:1024])
        bm = g.wst[:, 1, 0:512].rearrange("p (b t) -> p b t", b=NB)
        free = XL[:, :, :, :].rearrange("p v h t -> p (v h t)")
        CS = free[:, 0:2048].rearrange("p (b h v) -> p b h v", b=2, h=H)
        QB = free[:, 2048:2560].rearrange("p (b h t) -> p b h t", b=2, h=H)
        KB = free[0:TS, 2560:3584].rearrange("p (b h d) -> p b h d", b=2, h=H)
        s = {name: sc.sem(name) for name in ("consts", "args_ready", "kd_arg_ready", "level_exps_ready", "b_exps_ready", "kd_exp_ready",
                         "levels_ready", "q_ready", "k_ready", "k_turned", "k_copied", "v_turned", "v_copied",
                         "level_done", "level_merged", "merge_begun", "num_ready", "sq_ready", "ln_ready", "est_ready",
                         "small_steps", "yn_ready", "state_ready", "state_added", "y_turned", "y_gated",
                         "hi_ready", "lo_ready", "stored", "cleared", "qb_ready", "kb_ready", "b_inter",
                         "b_state", "b_added")}
        landed = [sc.sem("landed0"), sc.sem("landed1")]
        c_landed = [sc.sem("c_landed0"), sc.sem("c_landed1")]
        c_stored = [sc.sem("c_stored0"), sc.sem("c_stored1")]
        ps = g.ps
        sample = lambda c: isinstance(c, int) and c == NC
        size = lambda c: TS if sample(c) else L
        bank = lambda b, n=L: ps[:, b, :].rearrange("p (h t) -> p h t", h=H)[:, :, 0:n]
        S_in = a["state_gla_S"].rearrange("l b h d v -> (l b) d h v")
        S_out = a["S_sample"].rearrange("l b h d v -> (l b) d h v")
        levels_of = lambda c: range(4 if sample(c) else 0, NLV + 1)

        def halves(ap, n, half):
            return ap.rearrange("p h (b u t) -> p h b u t", u=2, t=n)[:, :, :, half, :]

        def store_state(sp, b):
            sp.wait_ge(s["b_added"], b + 1)
            sp.dma_start(S_out[b], CS[:, b % 2, :, :]).then_inc(c_stored[b % 2], 16)

        def everywhere(one):
            def run(eng):
                one(0, 0, 0)
                one(1, 0, 1)
                with eng.Fori(1, NC // 2) as i:
                    for par in range(2):
                        one(i * 2 + par, i, par)
            return run

        with nc.Block() as block:
            @block.sync
            def _(sp):
                sp.dma_start(masks[:, :, :], a["c_levels"]).then_inc(s["consts"], 16)
                sp.dma_start(bm, a["c_batch_cols"]).then_inc(s["consts"], 16)
                sp.dma_start(bmr[:, :], a["c_batch_rows"]).then_inc(s["consts"], 16)

                def load(c, half, par):
                    n = size(c)
                    wait(sp, s["y_gated"], c - 1)
                    sp.dma_start(inp[:, par, :, 0:n], g.PT[:, :, ds(c * L, n)].rearrange("m p t -> p m t")
                                 ).then_inc(landed[par], 16)
                everywhere(load)(sp)
                load(NC, NC // 2, 0)
                sp.wait_ge(s["state_added"], NC + 1)
                sp.dma_start(a["S_prompt"].rearrange("l b h d v -> (l b d) h v"), S[:, :, :]).then_inc(s["stored"], 16)
                sp.wait_ge(s["level_done"], (NLV + 1) * NC + 4)
                for b in range(NB):
                    if b >= 2:
                        sp.wait_ge(c_stored[b % 2], 16 * (b // 2))
                    sp.dma_start(CS[:, b % 2, :, :], S_in[b]).then_inc(c_landed[b % 2], 16)
                    if b >= 1:
                        store_state(sp, b - 1)
                store_state(sp, NB - 1)
                sp.wait_ge(s["stored"], 16)
                for par in range(2):
                    sp.wait_ge(c_stored[par], 16 * (NB // 2))

            @block.gpsimd
            def _(pool):
                def args(c, half, par):
                    n = size(c)
                    Bc = inp[:, par, 24:28, 0:n]
                    pool.wait_ge(landed[par], half * 16 + 16)
                    wait(pool, s["level_done"], c * (NLV + 1) if not sample(c) else (NLV + 1) * NC)
                    for v in levels_of(c):
                        if v == NLV:
                            continue
                        w = LEVELS[v]
                        nb = n // (2 * w)
                        mid = Bc.rearrange("p h (b u) -> p h b u", u=2 * w)[:, :, :, w - 1:w].to_broadcast([P, H, nb, w])
                        pool.tensor_tensor(halves(XL[:, v, :, 0:n], w, 0), mid, halves(Bc, w, 0), ALU.subtract)
                        ins = pool.tensor_tensor(halves(XL[:, v, :, 0:n], w, 1), halves(Bc, w, 1), mid, ALU.subtract)
                    ins.then_inc(s["args_ready"], 1)
                    wait(pool, s["k_turned"], c)
                    blk = DS if sample(c) else L
                    end = Bc.rearrange("p h (b u) -> p h b u", u=blk)
                    pool.tensor_tensor(KD[:, :, 0:n].rearrange("p h (b u) -> p h b u", u=blk),
                                       end[:, :, :, blk - 1:blk].to_broadcast([P, H, n // blk, blk]), end,
                                       ALU.subtract).then_inc(s["kd_arg_ready"], 1)

                def low(c):
                    n = size(c)
                    pool.wait_ge(s["hi_ready"], c + 1)
                    pool.tensor_tensor(g.HL[:, :, ds(c * L, n)], TT[:, :, 0:n],
                                       g.HH[:, :, ds(c * L, n)].bitcast(F32), ALU.subtract).then_inc(s["lo_ready"], 1)
                args(0, 0, 0)
                args(1, 0, 1)
                low(0)
                with pool.Fori(1, NC // 2) as i:
                    for par in range(2):
                        args(i * 2 + par, i, par)
                        low(i * 2 + (par - 1))
                args(NC, NC // 2, 0)
                low(NC - 1)
                low(NC)

            @block.scalar
            def _(act):
                def first(c, half, par):
                    n = size(c)
                    wait(act, s["state_added"], c + 1)
                    act.wait_ge(landed[par], half * 16 + 16)
                    act.activation(EB[:, :, 0:n], inp[:, par, 24:28, 0:n], ACT.Exp, scale=ITAU).then_inc(s["b_exps_ready"], 1)
                    act.wait_ge(s["kd_arg_ready"], c + 1)
                    act.activation(KD[:, :, 0:n], KD[:, :, 0:n], ACT.Exp, scale=ITAU).then_inc(s["kd_exp_ready"], 1)
                    v0 = 4 if sample(c) else 0
                    act.activation(XL[:, v0:NLV, :, 0:n], XL[:, v0:NLV, :, 0:n], ACT.Exp, scale=ITAU
                                   ).then_inc(s["level_exps_ready"], 1)
                    act.wait_ge(s["v_turned"], c + 1)
                    act.activation(VN[0:n, :, :], ps[0:n, 1:3, :].rearrange("p b (h v) -> p (b h) v", h=2),
                                   ACT.Copy).then_inc(s["v_copied"], 1)
                    act.wait_ge(s["k_turned"], c + 1)
                    act.activation(KN[0:n, :, :], bank(0)[0:n], ACT.Copy).then_inc(s["k_copied"], 1)

                def second(c, half, par):
                    n = size(c)
                    act.wait_ge(s["b_inter"] if sample(c) else s["num_ready"], NB if sample(c) else c + 1)
                    wait(act, s["y_turned"], c)
                    for h in range(H):
                        ins = act.activation(YN[0:n, h, :], ps[0:n, 4 + h, 0:DV], ACT.Square,
                                             accum_out=SM[0:n, 3, h:h + 1])
                    ins.then_inc(s["sq_ready"], 1)
                    act.wait_ge(s["sq_ready"], c + 1)
                    act.activation(SM[0:n, 4, :], SM[0:n, 3, :], ACT.Ln, bias=g.eps[0:n, 0:1], scale=1.0 / DV
                                   ).then_inc(s["ln_ready"], 1)
                    act.wait_ge(s["ln_ready"], c + 1)
                    act.activation(SM[0:n, 5, :], SM[0:n, 4, :], ACT.Exp, scale=-0.5).then_inc(s["est_ready"], 1)
                    act.wait_ge(s["y_gated"], c + 1)
                    act.activation(g.HH[:, :, ds(c * L, n)], TT[:, :, 0:n], ACT.Copy).then_inc(s["hi_ready"], 1)

                def both(c, half, par):
                    first(c, half, par)
                    second(c, half, par)
                everywhere(both)(act)
                both(NC, NC // 2, 0)

            @block.vector
            def _(dve):
                def first(c, half, par):
                    n = size(c)
                    q, k = inp[:, par, 0:H, 0:n], inp[:, par, H:2 * H, 0:n]
                    dve.wait_ge(s["b_exps_ready"], c + 1)
                    wait(dve, s["num_ready"], c)
                    dve.tensor_tensor(QE[:, :, 0:n], EB[:, :, 0:n], q, ALU.mult).then_inc(s["q_ready"], 1)
                    dve.wait_ge(s["kd_exp_ready"], c + 1)
                    dve.tensor_tensor(KD[:, :, 0:n], KD[:, :, 0:n], k, ALU.mult).then_inc(s["k_ready"], 1)
                    dve.wait_ge(s["level_exps_ready"], c + 1)
                    for v in levels_of(c):
                        if v == NLV:
                            continue
                        for half_, x in ((0, k), (1, q)):
                            dst = halves(XL[:, v, :, 0:n], LEVELS[v], half_)
                            ins = dve.tensor_tensor(dst, dst, halves(x, LEVELS[v], half_), ALU.mult)
                    ins.then_inc(s["levels_ready"], 1)
                    if sample(c):
                        dve.memset(A, 0.0).then_inc(s["cleared"], 1)
                        dve.wait_ge(s["cleared"], 2)
                    for j, v in enumerate(levels_of(c)):
                        done = (c * (NLV + 1) if not sample(c) else (NLV + 1) * NC) + (j + 1)
                        dve.wait_ge(s["level_done"], done)
                        if j or not (isinstance(c, int) and c == 0):
                            dve.wait_ge(s["level_merged"], done - 1)
                        dve.sem_inc(s["merge_begun"], 1)
                        dve.copy_predicated(A[0:n, :, 0:n], masks[0:n, v, 0:n].unsqueeze(1).to_broadcast([n, H, n]),
                                            bank((3 + j) % 4, n)[0:n]).then_inc(s["level_merged"], 1)

                def second(c, par):
                    n = size(c)
                    base = c * 4
                    dve.wait_ge(s["est_ready"], c + 1)
                    dve.tensor_scalar(SM[0:n, 6, :], SM[0:n, 3, :], 1.0 / DV, EPS, ALU.mult, ALU.add
                                      ).then_inc(s["small_steps"], 1)
                    dve.scalar_tensor_tensor(SM[0:n, 7, :], SM[0:n, 5, :], -0.5, SM[0:n, 5, :], ALU.mult, ALU.mult
                                             ).then_inc(s["small_steps"], 1)
                    dve.wait_ge(s["small_steps"], base + 2)
                    dve.tensor_tensor(SM[0:n, 6, :], SM[0:n, 7, :], SM[0:n, 6, :], ALU.mult).then_inc(s["small_steps"], 1)
                    dve.wait_ge(s["small_steps"], base + 3)
                    dve.scalar_tensor_tensor(SM[0:n, 7, :], SM[0:n, 6, :], 1.5, SM[0:n, 5, :], ALU.add, ALU.mult
                                             ).then_inc(s["small_steps"], 1)
                    dve.wait_ge(s["small_steps"], base + 4)
                    for h in range(H):
                        ins = dve.tensor_scalar(YN[0:n, h, :], ps[0:n, 4 + h, 0:DV], SM[0:n, 7, h:h + 1], None, ALU.mult)
                    ins.then_inc(s["yn_ready"], 1)

                def state(c):
                    dve.wait_ge(s["state_ready"], c + 1)
                    for h in range(H):
                        ins = dve.scalar_tensor_tensor(S[:, h, :], S[:, h, :], EB[:, h, L - 1:L], ps[:, h, 0:DV],
                                                       ALU.mult, ALU.add)
                    ins.then_inc(s["state_added"], 1)

                def gated(c, par):
                    n = size(c)
                    dve.wait_ge(s["y_turned"], c + 1)
                    wait(dve, s["lo_ready"], c)
                    dve.tensor_tensor(TT[:, :, 0:n], ps[:, 4:6, :].rearrange("p b (j t) -> p (b j) t", j=4)[:, :, 0:n],
                                      inp[:, par, 16:24, 0:n], ALU.mult).then_inc(s["y_gated"], 1)

                def chunk(c, half, par):
                    first(c, half, par)
                    second(c, par)
                    state(c)
                    gated(c, par)

                dve.memset(S[:, :, :], 0.0).then_inc(s["state_added"], 1)
                dve.memset(A, 0.0).then_inc(s["cleared"], 1)
                dve.wait_ge(s["cleared"], 1)
                dve.wait_ge(s["consts"], 48)
                everywhere(chunk)(dve)
                first(NC, NC // 2, 0)
                for b in range(NB):
                    wait(dve, s["b_inter"], b - 1)
                    dve.wait_ge(s["level_done"], (NLV + 1) * NC + 4)
                    dve.wait_ge(s["q_ready"], NC + 1)
                    dve.tensor_tensor(QB[:, b % 2, :, :], QE[:, :, 0:TS],
                                      bm[:, b, :].unsqueeze(1).to_broadcast([P, H, TS]), ALU.mult).then_inc(s["qb_ready"], 1)
                    wait(dve, s["b_state"], b - 1)
                    dve.wait_ge(s["k_copied"], NC + 1)
                    dve.tensor_scalar(KB[:, b % 2, :, :], KN[0:TS, :, :], bmr[:, b:b + 1], None, ALU.mult
                                      ).then_inc(s["kb_ready"], 1)
                    dve.wait_ge(s["b_state"], b + 1)
                    dve.wait_ge(s["b_inter"], b + 1)
                    for h in range(H):
                        t = b * DS + DS - 1
                        ins = dve.scalar_tensor_tensor(CS[:, b % 2, h, :], CS[:, b % 2, h, :],
                                                       EB[:, h, t:t + 1], ps[:, h, 0:DV], ALU.mult, ALU.add)
                    ins.then_inc(s["b_added"], 1)
                second(NC, 0)
                gated(NC, 0)

            @block.tensor
            def _(pe):
                def scores(c, half, par):
                    n = size(c)
                    x = inp[:, par, :, :]
                    pe.wait_ge(landed[par], half * 16 + 16)
                    pe.wait_ge(s["state_added"], c + 1)
                    for j in range(8):
                        mm = pe.transpose(ps[0:n, 1 + j // 4, (j % 4) * P:(j % 4 + 1) * P], x[:, 8 + j, 0:n],
                                          g.ident[:, :])
                    mm.then_inc(s["v_turned"], 1)
                    pe.wait_ge(s["k_ready"], c + 1)
                    for h in range(H):
                        mm = pe.transpose(ps[0:n, 0, h * L:(h + 1) * L], KD[:, h, 0:n], g.ident[:, :])
                    mm.then_inc(s["k_turned"], 1)
                    pe.wait_ge(s["levels_ready"], c + 1)
                    base = c * (NLV + 1) if not sample(c) else (NLV + 1) * NC
                    for j, v in enumerate(levels_of(c)):
                        if j == 1:
                            pe.wait_ge(s["k_copied"], c + 1)
                        if j == 2:
                            pe.wait_ge(s["v_copied"], c + 1)
                        if j >= 4:
                            pe.wait_ge(s["level_merged"], base + (j - 3))
                        for h in range(H):
                            lhs, rhs = (XL[:, v, h, 0:n],) * 2 if v < NLV else (x[:, H + h, 0:n], x[:, h, 0:n])
                            mm = pe.matmul(ps[0:n, (3 + j) % 4, h * L:h * L + n], lhs, rhs, start=True, stop=True)
                        mm.then_inc(s["level_done"], 1)
                    pe.wait_ge(s["level_merged"], base + len(levels_of(c)))

                def turn_y(c):
                    n = size(c)
                    pe.wait_ge(s["yn_ready"], c + 1)
                    for j in range(8):
                        mm = pe.transpose(ps[:, 4 + j // 4, (j % 4) * L:(j % 4) * L + n],
                                          YN[0:n, j // 2, (j % 2) * P:(j % 2 + 1) * P], g.ident[0:n, 0:n])
                    mm.then_inc(s["y_turned"], 1)

                def chunk(c, half, par):
                    scores(c, half, par)
                    wait(pe, s["y_gated"], c)
                    pe.wait_ge(s["q_ready"], c + 1)
                    for h in range(H):
                        pe.matmul(ps[:, 4 + h, 0:DV], QE[:, h, :], S[:, h, :], start=True, stop=False)
                        mm = pe.matmul(ps[:, 4 + h, 0:DV], A[:, h, :], VN[:, h, :], start=False, stop=True)
                    mm.then_inc(s["num_ready"], 1)
                    for h in range(H):
                        mm = pe.matmul(ps[:, h, 0:DV], KN[:, h, :], VN[:, h, :], start=True, stop=True)
                    mm.then_inc(s["state_ready"], 1)
                    turn_y(c)

                everywhere(chunk)(pe)
                scores(NC, NC // 2, 0)
                pe.wait_ge(s["y_gated"], NC)
                for h in range(H):
                    pe.matmul(ps[0:TS, 4 + h, 0:DV], A[0:TS, h, 0:TS], VN[0:TS, h, :], start=True, stop=False)
                for b in range(NB):
                    pe.wait_ge(c_landed[b % 2], 16 * (b // 2 + 1))
                    pe.wait_ge(s["qb_ready"], b + 1)
                    for h in range(H):
                        mm = pe.matmul(ps[0:TS, 4 + h, 0:DV], QB[:, b % 2, h, :], CS[:, b % 2, h, :],
                                       start=False, stop=(b == NB - 1))
                    mm.then_inc(s["b_inter"], 1)
                    pe.wait_ge(s["kb_ready"], b + 1)
                    wait(pe, s["b_added"], b)
                    for h in range(H):
                        mm = pe.matmul(ps[:, h, 0:DV], KB[:, b % 2, h, :], VN[0:TS, h, :], start=True, stop=True)
                    mm.then_inc(s["b_state"], 1)
                turn_y(NC)


def mixer_layer(nc, g, a, layer):
    mlstm = layer == 0
    w_in = a["w_in_mlstm"][0] if mlstm else a["w_in_gla"][0]
    wv = w_in.rearrange("(k p) e -> p k e", p=P)
    e0 = 2 * H * DQK + 2 * H * DV
    pre_norm(nc, g, f"pm{layer}", V_PRE_MIX + KD * layer)
    with Scope(nc, f"m{layer}") as sc:
        m = Globals()
        if mlstm:
            m.U = sc.sb("u", [H, TP])
            m.WI = sc.sb("wi", [H, TP])
            m.NAT = sc.sb("per_token", [P, NC + 1, 3 * H])
            m.DEC = sc.sb("decay", [P, NC + NB, H])
            extra = [(lambda w, k=k, r=r: w[:, k, r:r + H], wv[:, k, e0 + q * H:e0 + (q + 1) * H])
                     for k in range(KD) for q, r in enumerate((0, 32))]
        else:
            extra = [(lambda w: w[:, :, 0:16], wv[:, :, e0:e0 + 16])]
        with Scope(nc, f"g{layer}") as gs:
            GP = gs.sb("extra", [P, TP])
            proj_phase(nc, g, f"p{layer}", a, w_in, (1.0, QK_SCALE) if mlstm else (QK_SCALE, 1.0),
                       ACT.Sigmoid if mlstm else ACT.Silu, V_HEAD_M if mlstm else V_HEAD_G, extra, GP)
            if mlstm:
                gates_mlstm(nc, g, f"q{layer}", a, GP, m)
            else:
                gates_gla(nc, g, f"q{layer}", a, GP)
        if mlstm:
            mlstm_mix(nc, g, f"x{layer}", a, m)
        else:
            gla_mix(nc, g, f"x{layer}", a)
    with Scope(nc, f"m{layer}y") as sc:
        Y = sc.sb("Y", [P, KD, TP])
        wout_phase(nc, g, f"w{layer}", a["w_out_mlstm"][0] if mlstm else a["w_out_gla"][0], Y)
        post_norm(nc, g, f"qm{layer}", V_POST_MIX + KD * layer, Y)


def build(nc, a, parts):
    g = Globals()
    with ExitStack() as ctx:
        sb = lambda name, shape, dt=F32: ctx.enter_context(nc.sbuf_tensor(name, shape, dt))
        g.ps = ctx.enter_context(nc.psum_tensor("ps", [P, 8, 512], F32))
        g.X = sb("X", [P, KD, TP])
        g.HH = sb("HH", [P, KD, TP], F32R)
        g.HL = sb("HL", [P, KD, TP], F32R)
        g.wst = sb("w_stage", [P, 2, WCOLS])
        g.whi = sb("w_hi", [P, 2, WCOLS], F32R)
        g.wlo = sb("w_lo", [P, 2, WCOLS], F32R)
        g.ident = sb("ident", [P, P])
        g.ones = sb("ones", [P, P])
        g.vec = sb("vec", [P, NVEC])
        g.avg = sb("avg", [P, P])
        g.eps = sb("eps", [P, 1])
        g.reset = sb("reset", [P, TP])
        g.sel = sb("sel", [H, H, L])
        g.negi = sb("negi", [H, H])
        g.PT = nc.dram_tensor("proj_scratch", [28, P, TP], F32, kind="Internal").ap()
        g.const_loads = [(g.reset[:, :], a["c_reset"]), (g.sel[:, :, :], a["c_sel"]), (g.negi[:, :], a["c_negi"]),
                         (g.avg[:, :], a["c_avg"]), (g.eps[:, :], a["c_eps"]),
                         (g.ident[:, :], a["c_ident"]), (g.ones[:, :], a["c_ones"])]
        load_phase(nc, g, a)
        for layer in range(2):
            if f"mix{layer}" in parts:
                mixer_layer(nc, g, a, layer)
            if "ffn" in parts:
                pre_norm(nc, g, f"pf{layer}", V_PRE_FFN + KD * layer)
                with Scope(nc, f"f{layer}y") as sc:
                    Y = sc.sb("Y", [P, KD, TP])
                    ffn_phase(nc, g, f"f{layer}", layer, a, Y)
                    post_norm(nc, g, f"qf{layer}", V_POST_FFN + KD * layer, Y)
        store_phase(nc, g, a)


PARTS = ("mix0", "mix1", "ffn")
OUTS = [("y_prompt", (1, 1024, 1024)), ("y_sample", (8, 8, 1024)),
        ("C_prompt", (1, 1, 4, 128, 256)), ("n_prompt", (1, 1, 4, 128)), ("m_prompt", (1, 1, 4)),
        ("S_prompt", (1, 1, 4, 128, 256)), ("C_sample", (1, 8, 4, 128, 256)),
        ("n_sample", (1, 8, 4, 128)), ("m_sample", (1, 8, 4)), ("S_sample", (1, 8, 4, 128, 256))]


def constants():
    f = np.float32
    tok = np.arange(L)
    starts = np.ones(TP, f)
    starts[0:SEQ:L] = 0
    starts[SEQ:T:DS] = 0
    heads = np.eye(H, dtype=f)
    s, l = np.arange(L)[:, None], np.arange(L)[None, :]
    after = np.where(s <= l, 0.0, NEG).astype(f)
    s8, l8 = np.arange(TS)[:, None], np.arange(TS)[None, :]
    after8 = np.where((s8 <= l8) & (s8 // DS == l8 // DS), 0.0, NEG).astype(f)
    rows = (np.arange(TS)[:, None] // DS == np.arange(NB)[None, :]).astype(f)
    lv = []
    for w in (64, 32, 16, 8, 4, 2, 1):
        lv.append((s // (2 * w) == l // (2 * w)) & (s % (2 * w) < w) & (l % (2 * w) >= w))
    lv.append(s == l)
    c = {"c_levels": np.stack(lv, 1).astype(np.uint32), "c_reset": np.broadcast_to(starts, (P, TP)).copy(), "c_sel": np.repeat(heads[:, :, None], L, 2),
         "c_negi": -heads, "c_causal": after, "c_causal8": after8, "c_batch_rows": rows,
         "c_batch_cols": np.broadcast_to(rows.T, (P, NB, TS)).copy(),
         "c_ident": np.eye(P, dtype=f), "c_ones": np.ones((P, P), f),
         "c_avg": np.full((P, P), 1.0 / D, f), "c_eps": np.full((P, 1), EPS, f)}
    return c


def wanted(name):
    return name[0] == "y" or (name[0] in "Cnm" and "mix0" in PARTS) or (name[0] == "S" and "mix1" in PARTS)


def kernel(**inputs):
    import concourse.bacc as bacc
    from concourse.bass_utils import run_bass_kernel_spmd as run

    nc = bacc.Bacc("TRN2", target_bir_lowering=False, num_devices=1)
    arrays = {}
    a = {}
    for name, v in list(inputs.items()) + list(constants().items()):
        v = np.ascontiguousarray(v)
        arrays[f"{name}_in"] = v
        a[name] = nc.dram_tensor(f"{name}_in", v.shape, mybir.dt.from_np(v.dtype), kind="ExternalInput").ap()
    for name, shape in OUTS:
        if not wanted(name):
            continue
        a[name] = nc.dram_tensor(f"{name}_out", shape, F32, kind="ExternalOutput").ap()
    build(nc, a, PARTS)
    r = run(nc, [arrays], core_ids=[0])
    return tuple(r.results[0][f"{name}_out"] for name, _ in OUTS if wanted(name))
```

```python
from contextlib import ExitStack

import numpy as np

import concourse.bass as bass
from concourse import mybir

F32 = mybir.dt.float32
F32R = mybir.dt.float32r
U32 = mybir.dt.uint32
ALU = mybir.AluOpType
ACT = mybir.ActivationFunctionType
AX = mybir.AxisListType

P = 128
D = 1024
KD = D // P
SEQ = 1024
NB, DS = 8, 8
TS = NB * DS
T = SEQ + TS
GRP = 3
GT = 364
TP = GRP * GT
L = 128
NC = SEQ // L
H = 4
DQK = 128
DV = 256
DFF = 2816
KF = DFF // P
EPS = 1e-6
WCOLS = 1024
QK_SCALE = float(DQK) ** -0.5
NEG = -1.0e30
ds = bass.ds

V_PRE_MIX, V_POST_MIX, V_PRE_FFN, V_POST_FFN = 0, 16, 32, 48
V_HEAD_M, V_HEAD_G, V_BGATE = 64, 72, 80
NVEC = 84


def flat(ap):
    return ap.rearrange("p g t -> p (g t)")


class Globals:
    pass


class Scope:

    def __init__(self, nc, tag):
        self.nc, self.tag, self.ctx, self.sems = nc, tag, ExitStack(), []

    def sb(self, name, shape, dt=F32):
        return self.ctx.enter_context(self.nc.sbuf_tensor(f"{self.tag}_{name}", shape, dt))

    def sem(self, name):
        self.sems.append(self.nc.alloc_semaphore(f"{self.tag}_{name}"))
        return self.sems[-1]

    def __enter__(self):
        return self

    def __exit__(self, *a):
        if self.sems and a[0] is None:
            self.nc.clear_and_free_semaphores(self.sems)
            self.nc.all_engine_barrier()
        return self.ctx.__exit__(*a)



def weight_slots(sc, g):
    g.whi = sc.sb("w_hi", [P, 2, WCOLS], F32R)
    g.wlo = sc.sb("w_lo", [P, 2, WCOLS], F32R)
    w = Globals()
    w.landed = [sc.sem("w_landed0"), sc.sem("w_landed1")]
    w.hi, w.lo = sc.sem("w_hi_ready"), sc.sem("w_lo_ready")
    return w


def slot_load(sp, g, w, n, half, par, src, view=None):
    if not (isinstance(n, int) and n < 2):
        sp.wait_ge(w.lo, n - 1)
    dst = g.wst[:, par, :]
    if view is not None:
        dst = view(dst)
    sp.dma_start(dst, src).then_inc(w.landed[par], 16)


def slot_hi(act, g, w, half, par, units_done=None, need=None):
    act.wait_ge(w.landed[par], half * 16 + 16)
    if need is not None:
        act.wait_ge(units_done, need)
    act.activation(g.whi[:, par, :], g.wst[:, par, :], ACT.Copy).then_inc(w.hi, 1)


def slot_lo(dve, g, w, n, par):
    dve.wait_ge(w.hi, n + 1)
    dve.tensor_tensor(g.wlo[:, par, :], g.wst[:, par, :], g.whi[:, par, :].bitcast(F32),
                      ALU.subtract).then_inc(w.lo, 1)


def products(pe, g, bank0, hi, lo, par, wsl, ks, normed=None):
    mm = None
    for n, k in enumerate(ks):
        wh, wl = wsl(g.whi[:, par, :], k), wsl(g.wlo[:, par, :], k)
        if normed is not None:
            pe.wait_ge(normed, n + 1)
        for m, (wt, x) in enumerate(((wl, hi), (wh, hi), (wh, lo))):
            for t in range(GRP):
                mm = pe.matmul(g.ps[:, bank0 + t, 0:GT], wt, x[:, k, t * GT:(t + 1) * GT],
                               start=(n == 0 and m == 0), stop=(n == len(ks) - 1 and m == 2))
    return mm


def load_phase(nc, g, a):
    with Scope(nc, "in") as sc:
        xin = sc.sb("xrow", [P, 2, D])
        vrow = sc.sb("vrow", [NVEC, P])
        s_c = sc.sem("consts_landed")
        s_pad = sc.sem("pad_cleared")
        s_x = [sc.sem("x_landed0"), sc.sem("x_landed1")]
        s_t = sc.sem("x_turned")
        s_e = sc.sem("x_stored_act")
        s_f = sc.sem("x_stored_dve")
        s_v = sc.sem("vectors_turned")
        sq = sc.sb("sq", [P, 2, TP])
        s_sq, s_acc = sc.sem("squared"), sc.sem("summed")
        with nc.Block() as block:
            @block.sync
            def _(sp):
                for ap, src in g.const_loads:
                    sp.dma_start(ap, src).then_inc(s_c, 16)
                for r, src in ((V_PRE_MIX, a["g_pre_mix"]), (V_POST_MIX, a["g_post_mix"]),
                               (V_PRE_FFN, a["g_pre_ffn"]), (V_POST_FFN, a["g_post_ffn"]),
                               (V_HEAD_M, a["g_head_mlstm"]), (V_HEAD_G, a["g_head_gla"]),
                               (V_BGATE, a["b_gate_gla"])):
                    rows = src.rearrange("l (k p) -> (l k) p", p=P)
                    sp.dma_start(vrow[r:r + rows.shape[0], :], rows).then_inc(s_c, 16)
                for c in range(NC + 1):
                    if c >= 2:
                        sp.wait_ge(s_t, 2 * c - 2)
                    if c < NC:
                        sp.dma_start(xin[:, c % 2, :], a["x_prompt"][0, c * L:(c + 1) * L, :]
                                     ).then_inc(s_x[c % 2], 16)
                    else:
                        sp.dma_start(xin[0:TS, 0, :], a["x_sample"].rearrange("b s d -> (b s) d")
                                     ).then_inc(s_x[0], 16)

            @block.tensor
            def _(pe):
                pe.wait_ge(s_c, 16 * (len(g.const_loads) + 7))
                pe.transpose(g.ps[:, 7, 0:NVEC], vrow[:, :], g.ident[0:NVEC, 0:NVEC]).then_inc(s_v, 1)
                for c in range(NC + 1):
                    n = L if c < NC else TS
                    pe.wait_ge(s_x[c % 2], 16 * (c // 2 + 1))
                    for half, stored in ((0, s_e), (1, s_f)):
                        b = 2 * (c % 2) + half
                        if c >= 2:
                            pe.wait_ge(stored, c - 1)
                        for k in range(4):
                            mm = pe.transpose(g.ps[:, b, k * L:k * L + n],
                                              xin[0:n, c % 2, (4 * half + k) * P:(4 * half + k + 1) * P],
                                              g.ident[0:n, 0:n])
                        mm.then_inc(s_t, 1)

            def store(c, half):
                n = L if c < NC else TS
                dst = g.X[:, 4 * half:4 * half + 4, c * L:c * L + n]
                return dst, g.ps[:, 2 * (c % 2) + half, :].rearrange("p (k t) -> p k t", k=4)[:, :, 0:n]

            @block.scalar
            def _(act):
                for c in range(NC + 1):
                    act.wait_ge(s_t, 2 * c + 1)
                    act.activation(*store(c, 0), ACT.Copy).then_inc(s_e, 1)
                act.wait_ge(s_e, NC + 1)
                act.wait_ge(s_f, NC + 1)
                act.wait_ge(s_pad, 1)
                for k in range(KD):
                    square(act, sq, g.X[:, k, :], k, s_sq, s_acc)

            @block.vector
            def _(dve):
                dve.memset(g.X[:, :, T:TP], 0.0).then_inc(s_pad, 1)
                dve.wait_ge(s_v, 1)
                dve.tensor_copy(g.vec[:, :], g.ps[:, 7, 0:NVEC]).then_inc(s_pad, 1)
                for c in range(NC + 1):
                    dve.wait_ge(s_t, 2 * c + 2)
                    dve.tensor_copy(*store(c, 1)).then_inc(s_f, 1)
                for k in range(KD):
                    sum_up(dve, g, sq, k, s_sq, s_acc)


def by_group(ap):
    return ap.rearrange("p (g t) -> p g t", g=GRP)


def rstd_act(act, g, R, acc, s_ss, s_r):
    act.wait_ge(s_ss, 1)
    act.activation(by_group(acc[:, :]), g.ps[:, 0:GRP, 0:GT], ACT.Ln, bias=g.eps[:, 0:1]).then_inc(s_r, 1)
    act.wait_ge(s_r, 1)
    act.activation(R, acc[:, :], ACT.Exp, scale=-0.5).then_inc(s_r, 1)


def rstd_dve(dve, g, R, acc, s_r):
    dve.wait_ge(s_r, 2)
    dve.scalar_tensor_tensor(acc[:, :], R, -0.5, R, ALU.mult, ALU.mult).then_inc(s_r, 1)
    dve.wait_ge(s_r, 3)
    dve.scalar_tensor_tensor(by_group(acc[:, :]), g.ps[:, 0:GRP, 0:GT], EPS, by_group(acc[:, :]),
                             ALU.add, ALU.mult).then_inc(s_r, 1)
    dve.wait_ge(s_r, 4)
    dve.scalar_tensor_tensor(R, acc[:, :], 1.5, R, ALU.add, ALU.mult).then_inc(s_r, 1)
    dve.wait_ge(s_r, 5)


def square(act, sq, src, k, s_sq, s_acc):
    if k >= 2:
        act.wait_ge(s_acc, k - 1)
    act.activation(sq[:, k % 2, :], src, ACT.Square).then_inc(s_sq, 1)


def sum_up(dve, g, sq, k, s_sq, s_acc):
    dve.wait_ge(s_sq, k + 1)
    if k == 0:
        dve.tensor_copy(g.acc[:, :], sq[:, 0, :]).then_inc(s_acc, 1)
    else:
        dve.wait_ge(s_acc, k)
        dve.tensor_tensor(g.acc[:, :], g.acc[:, :], sq[:, k % 2, :], ALU.add).then_inc(s_acc, 1)


def col_means(pe, g, s_ss):
    for j in range(GRP):
        mm = pe.matmul(g.ps[:, j, 0:GT], g.avg[:, :], g.acc[:, j * GT:(j + 1) * GT], start=True, stop=True)
    mm.then_inc(s_ss, 1)


class PreNorm:

    def __init__(self, sc, g, col, t, R):
        self.g, self.col, self.t, self.R = g, col, t, R
        self.s_ss, self.s_r, self.s_t, self.s_hi, self.s_lo = (sc.sem(n) for n in (
            "col_sums", "rstd_steps", "normed", "norm_hi_ready", "norm_lo_ready"))

    def tensor(self, pe):
        col_means(pe, self.g, self.s_ss)

    def scalar(self, act):
        g = self.g
        rstd_act(act, g, self.R, g.acc, self.s_ss, self.s_r)
        for k in range(KD):
            act.wait_ge(self.s_t, k + 1)
            act.activation(g.HH[:, k, :], self.t[:, k % 2, :], ACT.Copy).then_inc(self.s_hi, 1)

    def vector(self, dve):
        g, col = self.g, self.col
        rstd_dve(dve, g, self.R, g.acc, self.s_r)
        for k in range(KD):
            if k >= 2:
                dve.wait_ge(self.s_lo, k - 1)
            dve.scalar_tensor_tensor(self.t[:, k % 2, :], g.X[:, k, :], g.vec[:, col + k:col + k + 1],
                                     self.R, ALU.mult, ALU.mult).then_inc(self.s_t, 1)

    def gpsimd(self, pool):
        g = self.g
        for k in range(KD):
            pool.wait_ge(self.s_hi, k + 1)
            pool.tensor_tensor(g.HL[:, k, :], self.t[:, k % 2, :], g.HH[:, k, :].bitcast(F32),
                               ALU.subtract).then_inc(self.s_lo, 1)


def post_norm(nc, g, tag, col, Y, last=False):
    with Scope(nc, tag) as sc:
        sq = sc.sb("sq", [P, 2, TP])
        R = sc.sb("rstd", [P, TP])
        s_sq, s_acc, s_ss, s_r = (sc.sem(n) for n in ("squared", "summed", "col_sums", "rstd_steps"))
        s_t, s_x = (sc.sem(n) for n in ("normed", "x_added"))
        with nc.Block() as block:
            @block.scalar
            def _(act):
                act.preload_act_table_set("natural_log_exp_and_others")
                rstd_act(act, g, R[:, :], g.acc, s_ss, s_r)
                if not last:
                    for k in range(KD):
                        act.wait_ge(s_x, k + 1)
                        square(act, sq, g.X[:, k, :], k, s_sq, s_acc)

            @block.tensor
            def _(pe):
                col_means(pe, g, s_ss)

            @block.vector
            def _(dve):
                rstd_dve(dve, g, R[:, :], g.acc, s_r)
                for k in range(KD):
                    dve.scalar_tensor_tensor(Y[:, k, :], Y[:, k, :], g.vec[:, col + k:col + k + 1],
                                             R[:, :], ALU.mult, ALU.mult).then_inc(s_t, 1)
                    if k >= 2 and not last:
                        sum_up(dve, g, sq, k - 2, s_sq, s_acc)
                if not last:
                    for k in (KD - 2, KD - 1):
                        sum_up(dve, g, sq, k, s_sq, s_acc)

            @block.gpsimd
            def _(pool):
                for k in range(KD):
                    pool.wait_ge(s_t, k + 1)
                    pool.tensor_tensor(g.X[:, k, :], g.X[:, k, :], Y[:, k, :], ALU.add).then_inc(s_x, 1)


def store_phase(nc, g, a):
    with Scope(nc, "out") as sc:
        yrow = sc.sb("yrow", [P, 2, D])
        s_t, s_e, s_f = (sc.sem(n) for n in ("y_turned", "y_copied_act", "y_copied_dve"))
        s_o = [sc.sem("y_stored0"), sc.sem("y_stored1")]
        with nc.Block() as block:
            @block.tensor
            def _(pe):
                for c in range(NC + 1):
                    n = L if c < NC else TS
                    for half, copied in ((0, s_e), (1, s_f)):
                        b = 2 * (c % 2) + half
                        if c >= 2:
                            pe.wait_ge(copied, c - 1)
                        for k in range(4):
                            mm = pe.transpose(g.ps[0:n, b, k * P:(k + 1) * P],
                                              g.X[:, 4 * half + k, c * L:c * L + n], g.ident[:, :])
                        mm.then_inc(s_t, 1)

            @block.scalar
            def _(act):
                for c in range(NC + 1):
                    n = L if c < NC else TS
                    act.wait_ge(s_t, 2 * c + 1)
                    if c >= 2:
                        act.wait_ge(s_o[c % 2], 16 * (c // 2))
                    act.activation(yrow[0:n, c % 2, 0:512], g.ps[0:n, 2 * (c % 2), :], ACT.Copy).then_inc(s_e, 1)

            @block.vector
            def _(dve):
                for c in range(NC + 1):
                    n = L if c < NC else TS
                    dve.wait_ge(s_t, 2 * c + 2)
                    if c >= 2:
                        dve.wait_ge(s_o[c % 2], 16 * (c // 2))
                    dve.tensor_copy(yrow[0:n, c % 2, 512:D], g.ps[0:n, 2 * (c % 2) + 1, :]).then_inc(s_f, 1)

            @block.sync
            def _(sp):
                for c in range(NC + 1):
                    sp.wait_ge(s_e, c + 1)
                    sp.wait_ge(s_f, c + 1)
                    if c < NC:
                        sp.dma_start(a["y_prompt"][0, c * L:(c + 1) * L, :], yrow[:, c % 2, :]
                                     ).then_inc(s_o[c % 2], 16)
                    else:
                        sp.dma_start(a["y_sample"].rearrange("b s d -> (b s) d"), yrow[0:TS, 0, :]
                                     ).then_inc(s_o[0], 16)
                sp.wait_ge(s_o[0], 16 * (NC // 2 + 1))
                sp.wait_ge(s_o[1], 16 * (NC // 2))


def ffn_phase(nc, g, tag, layer, a, Y, norm_col):
    NBLK = KF // 2
    LAST = NBLK - 1
    wg = a["w_ffn_gate"][layer].rearrange("(k p) f -> p k f", p=P)
    wu = a["w_ffn_up"][layer].rearrange("(k p) f -> p k f", p=P)
    wd = a["w_ffn_down"][layer].rearrange("(k p) d -> p k d", p=P)
    cols8 = lambda w, k: w[:, k * P:(k + 1) * P]
    slot8 = lambda w: w.rearrange("p (k m) -> p k m", k=KD)
    slot2 = lambda w: w.rearrange("p (k m) -> p k m", k=2)

    with Scope(nc, tag) as sc:
        hh = sc.sb("hid_hi", [P, 2, TP], F32R)
        hl = sc.sb("hid_lo", [P, 2, TP], F32R)
        sg = sc.sb("silu", [P, 2, TP])
        pr = sc.sb("hid", [P, TP])
        w = weight_slots(sc, g)
        s_unit, s_silu, s_prod, s_hh, s_hl = (sc.sem(n) for n in (
            "units_done", "silu_done", "hid_done", "hid_hi_ready", "hid_lo_ready"))
        norm = PreNorm(sc, g, norm_col, sg, pr[:, :])
        s_sq, s_acc = sc.sem("squared"), sc.sem("summed")
        s_y = sc.sem("y_cleared_and_down_added")
        unit0 = lambda i: i * 12 + 4
        slot0 = lambda i: i * 6 + 4
        half0 = lambda i: i * 3 + 2
        banks = lambda b0: g.ps[:, b0:b0 + GRP, 0:GT]
        grp = lambda ap: ap.rearrange("p (g t) -> p g t", g=GRP)

        with nc.Block() as block:
            @block.sync
            def _(sp):
                def load(n, half, par, kind, b, c=0):
                    if kind == "down":
                        slot_load(sp, g, w, n, half, par, wd[:, ds(b * 2, 2), c * 512:(c + 1) * 512], slot2)
                    else:
                        src = wg if kind == "gate" else wu
                        slot_load(sp, g, w, n, half, par, src[:, :, ds((b * 2 + c) * P, P)], slot8)
                for n, (kind, c) in enumerate((("gate", 0), ("up", 0), ("gate", 1), ("up", 1))):
                    load(n, n // 2, n % 2, kind, 0, c)
                with sp.Fori(0, LAST) as i:
                    for j, (kind, b, c) in enumerate((("gate", i + 1, 0), ("down", i, 0), ("down", i, 1),
                                                      ("up", i + 1, 0), ("gate", i + 1, 1), ("up", i + 1, 1))):
                        load(slot0(i) + j, half0(i) + j // 2, j % 2, kind, b, c)
                for c in range(2):
                    load(slot0(LAST) + c, half0(LAST), c, "down", LAST, c)

            @block.tensor
            def _(pe):
                def tile(n, par, bank0, normed=None):
                    pe.wait_ge(w.lo, n + 1)
                    products(pe, g, bank0, g.HH, g.HL, par, cols8, range(KD), normed).then_inc(s_unit, 1)

                def down(n, par, m0, i):
                    pe.wait_ge(w.lo, n + 1)
                    for m in range(m0, m0 + 4):
                        if m == 0:
                            pe.wait_ge(s_hl, i * 2 + 2)
                        elif m == 1:
                            pe.wait_ge(s_silu, 2 * NBLK if i is LAST else i * 2 + 3)
                        else:
                            pe.wait_ge(s_y, i * 8 + m)
                        q = m - m0
                        products(pe, g, 0 if m % 2 else 3, hh, hl, par,
                                 lambda w, k: w[:, k * 512 + q * P:k * 512 + (q + 1) * P],
                                 range(2)).then_inc(s_unit, 1)

                norm.tensor(pe)
                tile(0, 0, 0, norm.s_lo)
                tile(1, 1, 3)
                pe.wait_ge(s_silu, 1)
                tile(2, 0, 0)
                pe.wait_ge(s_prod, 1)
                tile(3, 1, 3)
                with pe.Fori(0, LAST) as i:
                    pe.wait_ge(s_silu, i * 2 + 2)
                    tile(slot0(i), 0, 0)
                    down(slot0(i) + 1, 1, 0, i)
                    down(slot0(i) + 2, 0, 4, i)
                    pe.wait_ge(s_y, i * 8 + 8)
                    tile(slot0(i) + 3, 1, 3)
                    pe.wait_ge(s_y, i * 8 + 9)
                    tile(slot0(i) + 4, 0, 0)
                    pe.wait_ge(s_prod, i * 2 + 3)
                    tile(slot0(i) + 5, 1, 3)
                down(slot0(LAST), 0, 0, LAST)
                down(slot0(LAST) + 1, 1, 4, LAST)

            @block.scalar
            def _(act):
                def silu(c, unit, before=None):
                    act.wait_ge(s_unit, unit + 1)
                    if before is not None:
                        act.wait_ge(s_prod, before)
                    act.activation(grp(sg[:, c, :]), banks(0), ACT.Silu).then_inc(s_silu, 1)

                def hid_hi(c, count, downs=None):
                    act.wait_ge(s_prod, count)
                    if downs is not None:
                        act.wait_ge(s_unit, downs)
                    act.activation(hh[:, c, :], pr[:, :], ACT.Copy).then_inc(s_hh, 1)

                slot_hi(act, g, w, 0, 0)
                slot_hi(act, g, w, 0, 1)
                act.preload_act_table_set("natural_log_exp_and_others")
                norm.scalar(act)
                silu(0, 0)
                slot_hi(act, g, w, 1, 0, s_unit, 1)
                slot_hi(act, g, w, 1, 1, s_unit, 2)
                hid_hi(0, 1)
                silu(1, 2)
                slot_hi(act, g, w, half0(0), 0, s_unit, 3)
                hid_hi(1, 2)
                with act.Fori(0, LAST) as i:
                    u = unit0(i)
                    slot_hi(act, g, w, half0(i), 1, s_unit, u)
                    silu(0, u, i * 2 + 1)
                    slot_hi(act, g, w, half0(i) + 1, 0, s_unit, u + 1)
                    slot_hi(act, g, w, half0(i) + 1, 1, s_unit, u + 5)
                    slot_hi(act, g, w, half0(i) + 2, 0, s_unit, u + 9)
                    hid_hi(0, i * 2 + 3, u + 9)
                    slot_hi(act, g, w, half0(i) + 2, 1, s_unit, u + 10)
                    silu(1, u + 10, i * 2 + 2)
                    slot_hi(act, g, w, half0(i) + 3, 0, s_unit, u + 11)
                    hid_hi(1, i * 2 + 4)
                slot_hi(act, g, w, half0(LAST), 1, s_unit, unit0(LAST))
                for m in range(8):
                    act.wait_ge(s_y, LAST * 8 + m + 2)
                    square(act, sg, Y[:, m, :], m, s_sq, s_acc)

            @block.vector
            def _(dve):
                def product(c, unit, count):
                    dve.wait_ge(s_unit, unit + 1)
                    dve.wait_ge(s_silu, count + 1)
                    if not (isinstance(count, int) and count == 0):
                        dve.wait_ge(s_hl, count)
                    dve.tensor_tensor(grp(pr[:, :]), banks(3), grp(sg[:, c, :]), ALU.mult).then_inc(s_prod, 1)
                    dve.wait_ge(s_hh, count + 1)
                    dve.tensor_tensor(hl[:, c, :], pr[:, :], hh[:, c, :].bitcast(F32),
                                      ALU.subtract).then_inc(s_hl, 1)

                def add(m, unit, count):
                    dve.wait_ge(s_unit, unit + 1)
                    dve.wait_ge(s_y, count + 1)
                    dve.tensor_tensor(grp(Y[:, m, :]), banks(0 if m % 2 else 3), grp(Y[:, m, :]),
                                      ALU.add).then_inc(s_y, 1)

                slot_lo(dve, g, w, 0, 0)
                slot_lo(dve, g, w, 1, 1)
                norm.vector(dve)
                slot_lo(dve, g, w, 2, 0)
                slot_lo(dve, g, w, 3, 1)
                product(0, 1, 0)
                slot_lo(dve, g, w, 4, 0)
                product(1, 3, 1)
                with dve.Fori(0, LAST) as i:
                    u = unit0(i)
                    slot_lo(dve, g, w, slot0(i) + 1, 1)
                    slot_lo(dve, g, w, slot0(i) + 2, 0)
                    for m in range(4):
                        add(m, u + (1 + m), i * 8 + m)
                    slot_lo(dve, g, w, slot0(i) + 3, 1)
                    for m in range(4, 8):
                        add(m, u + (1 + m), i * 8 + m)
                    slot_lo(dve, g, w, slot0(i) + 4, 0)
                    product(0, u + 9, i * 2 + 2)
                    slot_lo(dve, g, w, slot0(i) + 5, 1)
                    slot_lo(dve, g, w, slot0(i) + 6, 0)
                    product(1, u + 11, i * 2 + 3)
                slot_lo(dve, g, w, slot0(LAST) + 1, 1)
                for m in range(8):
                    add(m, unit0(LAST) + m, LAST * 8 + m)
                    if m:
                        sum_up(dve, g, sg, m - 1, s_sq, s_acc)
                sum_up(dve, g, sg, 7, s_sq, s_acc)

            @block.gpsimd
            def _(pool):
                norm.gpsimd(pool)
                pool.memset(Y[:, :, :], 0.0).then_inc(s_y, 1)


def wait(eng, sem, value):
    if not (isinstance(value, int) and value <= 0):
        eng.wait_ge(sem, value)


cols8 = lambda w, k: w[:, k * P:(k + 1) * P]
slot8 = lambda w: w.rearrange("p (k m) -> p k m", k=KD)


def proj_phase(nc, g, tag, a, w_in, qk_scales, gate_fn, head_col, extra_loads, GP, norm_col):
    NU = 24
    wv = w_in.rearrange("(k p) e -> p k e", p=P)
    with Scope(nc, tag) as sc:
        ob = sc.sb("out", [P, 2, TP])
        w = weight_slots(sc, g)
        t, R = sc.sb("normed", [P, 2, TP]), sc.sb("rstd", [P, TP])
        norm = PreNorm(sc, g, norm_col, t, R[:, :])
        s_unit, s_copied, s_gated = (sc.sem(n) for n in ("units_done", "psum_copied", "gated"))
        s_stored = [sc.sem("stored0"), sc.sem("stored1")]
        s_z, s_e = sc.sem("extra_cleared"), sc.sem("extra_landed")
        with nc.Block() as block:
            @block.sync
            def _(sp):
                def load(n, half, par):
                    sp.wait_ge(w.lo, n + 1)
                    sp.dma_start(slot8(g.wst[:, par, :]), wv[:, :, ds(n * P, P)]).then_inc(w.landed[par], 16)

                def store(u, par, ready, count):
                    sp.wait_ge(ready, count)
                    sp.dma_start(g.PT[ds(u, 1), :, :].rearrange("m p t -> (m p) t"), ob[:, par, :]
                                 ).then_inc(s_stored[par], 16)

                for par in range(2):
                    sp.sem_inc(s_stored[par], 16)
                    load(par, 0, par)
                with sp.Fori(0, 8) as i:
                    for j in range(2):
                        load(i * 2 + (j + 2), i + 1, j)
                        store(i * 2 + j, j, s_copied, i * 2 + (j + 3))
                with sp.Fori(8, 11) as i:
                    for j in range(2):
                        load(i * 2 + (j + 2), i + 1, j)
                        store(i * 2 + j, j, s_gated, i * 2 + (j - 15))
                sp.wait_ge(s_z, 1)
                for dst, src in extra_loads:
                    sp.dma_start(dst(slot8(g.wst[:, 0, :])), src).then_inc(s_e, 16)
                for j in range(2):
                    store(22 + j, j, s_gated, 7 + j)
                for par in range(2):
                    sp.wait_ge(s_stored[par], 16 * (NU // 2 + 1))

            @block.gpsimd
            def _(pool):
                norm.gpsimd(pool)
                pool.wait_ge(w.lo, NU - 1 + 2)
                pool.memset(g.wst[:, 0, :], 0.0).then_inc(s_z, 1)

            @block.tensor
            def _(pe):
                pe.sem_inc(s_unit, 2)

                def unit(u, par, normed=None):
                    pe.wait_ge(w.lo, u + 3)
                    pe.wait_ge(s_copied, u + 1)
                    products(pe, g, 3 * par, g.HH, g.HL, par, cols8, range(KD), normed).then_inc(s_unit, 1)
                norm.tensor(pe)
                unit(0, 0, norm.s_lo)
                unit(1, 1)
                with pe.Fori(1, NU // 2) as i:
                    for j in range(2):
                        unit(i * 2 + j, j)
                unit(NU, 0)

            @block.scalar
            def _(act):
                act.sem_inc(s_copied, 2)

                def hi(n, half, par):
                    act.wait_ge(w.landed[par], half * 16 + 16)
                    act.wait_ge(s_unit, n + 1)
                    act.activation(g.whi[:, par, :], g.wst[:, par, :], ACT.Copy).then_inc(w.hi, 1)

                def copy(u, half, par, func, scale=1.0):
                    act.wait_ge(s_unit, u + 3)
                    act.wait_ge(s_stored[par], half * 16 + 16)
                    act.activation(by_group(ob[:, par, :]), g.ps[:, 3 * par:3 * par + 3, 0:GT], func,
                                   scale=scale).then_inc(s_copied, 1)
                hi(0, 0, 0)
                act.preload_act_table_set("natural_log_exp_and_others")
                norm.scalar(act)
                for i0, i1, func, scale in ((0, 2, ACT.Copy, qk_scales[0]), (2, 4, ACT.Copy, qk_scales[1]),
                                            (4, 8, ACT.Copy, 1.0), (8, 11, gate_fn, 1.0)):
                    with act.Fori(i0, i1) as i:
                        hi(i * 2 + 1, i, 1)
                        copy(i * 2, i, 0, func, scale)
                        hi(i * 2 + 2, i + 1, 0)
                        copy(i * 2 + 1, i, 1, func, scale)
                hi(23, 11, 1)
                copy(22, 11, 0, gate_fn)
                act.wait_ge(s_e, 16 * len(extra_loads))
                act.wait_ge(s_unit, NU + 1)
                act.activation(g.whi[:, 0, :], g.wst[:, 0, :], ACT.Copy).then_inc(w.hi, 1)
                copy(23, 11, 1, gate_fn)
                act.wait_ge(s_unit, NU + 3)
                act.activation(by_group(GP[:, :]), g.ps[:, 0:3, 0:GT], ACT.Copy).then_inc(s_copied, 1)

            @block.vector
            def _(dve):
                dve.sem_inc(w.lo, 2)

                def lo(n, par):
                    dve.wait_ge(w.hi, n + 1)
                    dve.tensor_tensor(g.wlo[:, par, :], g.wst[:, par, :], g.whi[:, par, :].bitcast(F32),
                                      ALU.subtract).then_inc(w.lo, 1)
                lo(0, 0)
                norm.vector(dve)
                with dve.Fori(0, 8) as i:
                    lo(i * 2 + 1, 1)
                    lo(i * 2 + 2, 0)

                def gain(u, par, col):
                    dve.wait_ge(s_copied, u + 3)
                    dve.tensor_scalar(ob[:, par, :], ob[:, par, :], g.vec[:, ds(col, 1)], None,
                                      ALU.mult).then_inc(s_gated, 1)
                with dve.Fori(0, 4) as i:
                    for j in range(2):
                        lo(i * 2 + (17 + j), 1 - j)
                        gain(i * 2 + (16 + j), j, i * 2 + (head_col + j))


def wout_phase(nc, g, tag, w_out, Y):
    wv = w_out.rearrange("(k p) e -> p k e", p=P)
    with Scope(nc, tag) as sc:
        w = weight_slots(sc, g)
        sq = sc.sb("sq", [P, 2, TP])
        s_unit, s_copied = sc.sem("units_done"), sc.sem("psum_copied")
        s_sq, s_acc = sc.sem("squared"), sc.sem("summed")
        with nc.Block() as block:
            @block.sync
            def _(sp):
                with sp.Fori(0, KD // 2) as i:
                    for par in range(2):
                        sp.wait_ge(w.lo, i * 2 + (par + 1))
                        sp.dma_start(slot8(g.wst[:, par, :]), wv[:, :, ds((i * 2 + par) * P, P)]
                                     ).then_inc(w.landed[par], 16)

            @block.tensor
            def _(pe):
                pe.sem_inc(s_unit, 2)
                with pe.Fori(0, KD // 2) as i:
                    for par in range(2):
                        pe.wait_ge(w.lo, i * 2 + (par + 3))
                        pe.wait_ge(s_copied, i * 2 + (par + 1))
                        products(pe, g, 3 * par, g.HH, g.HL, par, cols8, range(KD)).then_inc(s_unit, 1)

            @block.scalar
            def _(act):
                act.sem_inc(s_copied, 2)

                def hi(n, half, par):
                    act.wait_ge(w.landed[par], half * 16 + 16)
                    act.wait_ge(s_unit, n + 1)
                    act.activation(g.whi[:, par, :], g.wst[:, par, :], ACT.Copy).then_inc(w.hi, 1)

                def copy(u, par):
                    act.wait_ge(s_unit, u + 3)
                    act.wait_ge(s_acc, u + 1)
                    act.activation(by_group(sq[:, par, :]), g.ps[:, 3 * par:3 * par + 3, 0:GT], ACT.Square
                                   ).then_inc(s_sq, 1)
                    act.activation(by_group(Y[:, ds(u, 1), :].rearrange("p m t -> p (m t)")),
                                   g.ps[:, 3 * par:3 * par + 3, 0:GT], ACT.Copy).then_inc(s_copied, 1)
                hi(0, 0, 0)
                with act.Fori(0, KD // 2 - 1) as i:
                    hi(i * 2 + 1, i, 1)
                    copy(i * 2, 0)
                    hi(i * 2 + 2, i + 1, 0)
                    copy(i * 2 + 1, 1)
                hi(KD - 1, KD // 2 - 1, 1)
                copy(KD - 2, 0)
                copy(KD - 1, 1)

            @block.vector
            def _(dve):
                dve.sem_inc(w.lo, 2)
                dve.memset(g.acc[:, :], 0.0).then_inc(s_acc, 2)

                def lo(n, par):
                    dve.wait_ge(w.hi, n + 1)
                    dve.tensor_tensor(g.wlo[:, par, :], g.wst[:, par, :], g.whi[:, par, :].bitcast(F32),
                                      ALU.subtract).then_inc(w.lo, 1)

                def add(u, par):
                    dve.wait_ge(s_sq, u + 1)
                    dve.wait_ge(s_acc, u + 2)
                    dve.tensor_tensor(g.acc[:, :], g.acc[:, :], sq[:, par, :], ALU.add).then_inc(s_acc, 1)
                lo(0, 0)
                with dve.Fori(0, KD // 2 - 1) as i:
                    lo(i * 2 + 1, 1)
                    add(i * 2, 0)
                    lo(i * 2 + 2, 0)
                    add(i * 2 + 1, 1)
                lo(KD - 1, 1)
                add(KD - 2, 0)
                add(KD - 1, 1)


def chunk_io(c):
    return c * L, (TS if isinstance(c, int) and c == NC else L)


def cheads(ap):
    return ap.rearrange("p (h t) -> p h t", h=H)


def gates_mlstm(nc, g, tag, a, GP, m):
    with Scope(nc, tag) as sc:
        Z = sc.sb("z", [H, TP])
        I = sc.sb("i", [H, TP])
        T1 = sc.sb("t1", [H, TP])
        LF = sc.sb("lf", [H, TP])
        B = sc.sb("b", [H, TP])
        M = sc.sb("m", [H, TP])
        W = sc.sb("wrow", [H, TP])
        EM = sc.sb("negm", [H, TP])
        WS = sc.sb("wsrow", [H, TP])
        MP = sc.sb("m_before", [H, NC + NB])
        DL = sc.sb("declog", [H, NC + NB])
        DD = sc.sb("decdiag", [H, NC + NB, H])
        bi = sc.sb("bi", [H, 2])
        s_in, s_d, s_a, s_p, s_out = (sc.sem(n) for n in (
            "small_landed", "dve_steps", "act_steps", "turned", "m_stored"))
        steps = {"n": 0}

        def nat(n, c0, c1, q0, q1):
            return g.ps[0:n, 0, 0:(NC + 1) * 3 * H].rearrange("p (c q) -> p c q", c=NC + 1)[:, c0:c1, q0:q1]

        with nc.Block() as block:
            @block.sync
            def _(sp):
                sp.dma_start(bi[:, 0:1], a["b_i_mlstm"].rearrange("l h -> h l")).then_inc(s_in, 16)
                sp.dma_start(bi[:, 1:2], a["b_f_mlstm"].rearrange("l h -> h l")).then_inc(s_in, 16)
                sp.dma_start(MP[:, NC:NC + NB], a["state_mlstm_m"].rearrange("l b h -> (l h) b"),
                             allow_slow_non_contiguous=True).then_inc(s_in, 16)
                sp.wait_ge(s_d, 11)
                sp.dma_start(a["m_prompt"].rearrange("l b h -> (l h) b"), M[:, SEQ - 1:SEQ],
                             allow_slow_non_contiguous=True).then_inc(s_out, 16)
                sp.dma_start(a["m_sample"].rearrange("l b h -> (l h) b"), M[:, SEQ + DS - 1:T:DS],
                             allow_slow_non_contiguous=True).then_inc(s_out, 16)
                sp.wait_ge(s_out, 32)

            @block.vector
            def _(dve):
                def step(ins):
                    steps["n"] += 1
                    ins.then_inc(s_d, 1)
                    dve.wait_ge(s_d, steps["n"])
                dve.wait_ge(s_in, 48)
                step(dve.tensor_scalar(I[:, :], GP[0:H, :], bi[:, 0:1], None, ALU.add))
                step(dve.tensor_copy(Z[:, :], GP[32:32 + H, :]))
                step(dve.tensor_scalar(Z[:, :], Z[:, :], bi[:, 1:2], None, ALU.add))
                dve.wait_ge(s_a, 3)
                step(dve.scalar_tensor_tensor(LF[:, :], Z[:, :], 0.0, T1[:, :], ALU.min, ALU.subtract))
                step(dve.tensor_tensor_scan(B[:, :], g.reset[0:H, :], LF[:, :], 0.0, ALU.mult, ALU.add))
                dve.tensor_tensor_scan(M[:, 0:SEQ], LF[:, 0:SEQ], I[:, 0:SEQ], 0.0, ALU.add, ALU.max)
                for b in range(NB):
                    t0 = SEQ + b * DS
                    ins = dve.tensor_tensor_scan(M[:, t0:t0 + DS], LF[:, t0:t0 + DS], I[:, t0:t0 + DS],
                                                 MP[:, NC + b:NC + b + 1], ALU.add, ALU.max)
                step(ins)
                step(dve.memset(M[:, T:TP], 0.0))
                step(dve.memset(MP[:, 0:1], 0.0))
                step(dve.tensor_copy(MP[:, 1:NC], M[:, L - 1:SEQ - 1:L]))
                step(dve.tensor_tensor(m.U[:, :], B[:, :], M[:, :], ALU.subtract))
                step(dve.tensor_tensor(W[:, :], I[:, :], B[:, :], ALU.subtract))
                step(dve.tensor_tensor(m.WI[:, 0:SEQ].rearrange("p (c t) -> p c t", t=L),
                                       m.U[:, 0:SEQ].rearrange("p (c t) -> p c t", t=L),
                                       MP[:, 0:NC].unsqueeze(2).to_broadcast([H, NC, L]), ALU.add))
                step(dve.tensor_tensor(m.WI[:, SEQ:T].rearrange("p (c t) -> p c t", t=DS),
                                       m.U[:, SEQ:T].rearrange("p (c t) -> p c t", t=DS),
                                       MP[:, NC:NC + NB].unsqueeze(2).to_broadcast([H, NB, DS]), ALU.add))
                step(dve.tensor_tensor(WS[:, 0:SEQ].rearrange("p (c t) -> p c t", t=L),
                                       W[:, 0:SEQ].rearrange("p (c t) -> p c t", t=L),
                                       m.U[:, L - 1:SEQ:L].unsqueeze(2).to_broadcast([H, NC, L]), ALU.add))
                step(dve.tensor_tensor(WS[:, SEQ:T].rearrange("p (c t) -> p c t", t=DS),
                                       W[:, SEQ:T].rearrange("p (c t) -> p c t", t=DS),
                                       m.U[:, SEQ + DS - 1:T:DS].unsqueeze(2).to_broadcast([H, NB, DS]), ALU.add))
                step(dve.tensor_tensor(DL[:, 0:NC], m.U[:, L - 1:SEQ:L], MP[:, 0:NC], ALU.add))
                step(dve.tensor_tensor(DL[:, NC:NC + NB], m.U[:, SEQ + DS - 1:T:DS], MP[:, NC:NC + NB], ALU.add))
                step(dve.tensor_tensor(DD[:, :, :], DL[:, :].unsqueeze(2).to_broadcast([H, NC + NB, H]),
                                       g.ident[0:H, 0:H].unsqueeze(1).to_broadcast([H, NC + NB, H]), ALU.mult))
                dve.wait_ge(s_p, 1)
                dve.tensor_copy(m.NAT[:, 0:NC, 0:H], nat(P, 0, NC, 0, H))
                step(dve.tensor_copy(m.NAT[0:TS, NC:NC + 1, 0:H], nat(TS, NC, NC + 1, 0, H)))

            @block.scalar
            def _(act):
                act.preload_act_table_set("natural_log_exp_and_others")
                act.wait_ge(s_d, 3)
                act.activation(T1[:, :], Z[:, :], ACT.Abs).then_inc(s_a, 1)
                act.wait_ge(s_a, 1)
                act.activation(T1[:, :], T1[:, :], ACT.Exp, scale=-1.0).then_inc(s_a, 1)
                act.wait_ge(s_a, 2)
                act.activation(T1[:, :], T1[:, :], ACT.Ln, bias=1.0).then_inc(s_a, 1)
                act.wait_ge(s_d, 13)
                act.activation(m.WI[:, 0:T], m.WI[:, 0:T], ACT.Exp).then_inc(s_a, 1)
                act.wait_ge(s_p, 1)
                act.wait_ge(s_d, 19)
                act.activation(m.NAT[:, 0:NC, H:3 * H], nat(P, 0, NC, H, 3 * H), ACT.Exp)
                act.activation(m.NAT[0:TS, NC:NC + 1, H:3 * H], nat(TS, NC, NC + 1, H, 3 * H), ACT.Exp).then_inc(s_a, 1)
                act.activation(m.DEC[:, :, :], g.ps[:, 1, 0:(NC + NB) * H].rearrange(
                    "p (c h) -> p c h", h=H), ACT.Exp).then_inc(s_a, 1)

            @block.tensor
            def _(pe):
                pe.wait_ge(s_d, 18)
                for c in range(NC + 1):
                    n = L if c < NC else TS
                    for q, row in enumerate((W, EM, WS)):
                        scale = g.negi[:, :] if row is EM else g.ident[0:H, 0:H]
                        src = M if row is EM else row
                        pe.matmul(g.ps[0:n, 0, (c * 3 + q) * H:(c * 3 + q + 1) * H],
                                  src[:, c * L:c * L + n], scale, start=True, stop=True)
                pe.matmul(g.ps[:, 1, 0:(NC + NB) * H], g.ones[0:H, :],
                          DD[:, :, :].rearrange("p c h -> p (c h)"), start=True, stop=True).then_inc(s_p, 1)


def pipelined(eng, ahead, chunk):
    ahead(0, 0, 0)
    chunk(0, 0, (1, 0, 1))
    with eng.Fori(0, NC // 2 - 1) as i:
        chunk(i * 2 + 1, 1, (i * 2 + 2, i + 1, 0))
        chunk(i * 2 + 2, 0, (i * 2 + 3, i + 1, 1))
    chunk(NC - 1, 1, (NC, NC // 2, 0))


def mlstm_mix(nc, g, tag, a, m):
    with Scope(nc, tag) as sc:
        inp = sc.sb("qkvo", [P, 2, 24, L])
        VA = sc.sb("v_one", [P, H, DV + 1])
        KW = sc.sb("k_weighted", [P, H, DQK])
        QW = sc.sb("q_weighted", [P, H, L])
        E = sc.sb("decays", [P, H, L])
        A = sc.sb("scores", [P, H, L])
        YN = sc.sb("y_normed", [P, H, DV])
        TT = sc.sb("y_gated", [P, KD, L])
        C = sc.sb("state", [P, H, DV + 1])
        SM = sc.sb("small", [P, 8, H])
        mask = sc.sb("mask", [P, L])
        mask8 = sc.sb("mask8", [TS, TS])
        CS = sc.sb("sample_state", [P, 2, H, DV + 1])
        KB = g.wst[0:TS, 0, :].rearrange("p (b h d) -> p b h d", b=2, h=H)
        QB = g.wst[:, 1, 0:2 * H * TS].rearrange("p (b h t) -> p b h t", b=2, h=H)
        bm = g.wst[:, 1, 2 * H * TS:].rearrange("p (b t) -> p b t", b=NB)
        bmr = sc.sb("batch_rows", [TS, NB])
        names = ("consts", "k_turned", "v_turned", "s_ready", "u_ready", "wi_ready", "k_scaled", "v_copied",
                 "masked", "decays_ready", "scores_ready", "q_scaled", "num_ready", "sq_ready", "ln_ready",
                 "yn_ready", "state_ready", "state_added", "y_turned", "y_gated", "hi_ready", "lo_ready",
                 "small_steps", "newton_done", "scale_ready", "ones_ready", "stored", "est_ready", "qb_ready", "kb_ready", "b_inter", "b_state",
                 "b_added")
        s = {name: sc.sem(name) for name in names}
        landed = [sc.sem("landed0"), sc.sem("landed1")]
        c_landed = [sc.sem("c_landed0"), sc.sem("c_landed1")]
        c_stored = [sc.sem("c_stored0"), sc.sem("c_stored1")]
        ps = g.ps
        bank = lambda b, n=L: ps[:, b, :].rearrange("p (h t) -> p h t", h=H)[:, :, 0:n]

        def tokens(c):
            return ds(c * L, TS if isinstance(c, int) and c == NC else L)

        C_in = a["state_mlstm_C"].rearrange("l b h d v -> (l b) d h v")
        n_in = a["state_mlstm_n"].rearrange("l b h d -> (l b) d h")
        C_out = a["C_sample"].rearrange("l b h d v -> (l b) d h v")
        n_out = a["n_sample"].rearrange("l b h d -> (l b) d h")
        with nc.Block() as block:
            def store_state(sp, b):
                par = b % 2
                sp.wait_ge(s["b_added"], b + 1)
                sp.dma_start(C_out[b], CS[:, par, :, 0:DV]).then_inc(c_stored[par], 16)
                sp.dma_start(n_out[b].unsqueeze(2), CS[:, par, :, DV:DV + 1],
                             allow_slow_non_contiguous=True).then_inc(c_stored[par], 16)

            @block.sync
            def _(sp):
                sp.dma_start(mask[:, :], a["c_causal"]).then_inc(s["consts"], 16)
                sp.dma_start(mask8[:, :], a["c_causal8"]).then_inc(s["consts"], 16)
                sp.dma_start(bm[:, :, :], a["c_batch_cols"]).then_inc(s["consts"], 16)
                sp.dma_start(bmr[:, :], a["c_batch_rows"]).then_inc(s["consts"], 16)

                def load(c, half, par):
                    n = TS if isinstance(c, int) and c == NC else L
                    wait(sp, s["y_gated"], c - 1)
                    sp.dma_start(inp[:, par, :, 0:n], g.PT[0:24, :, ds(c * L, n)].rearrange("m p t -> p m t")
                                 ).then_inc(landed[par], 16)
                load(0, 0, 0)
                load(1, 0, 1)
                with sp.Fori(1, NC // 2) as i:
                    for par in range(2):
                        load(i * 2 + par, i, par)
                load(NC, NC // 2, 0)
                sp.wait_ge(s["state_added"], NC + 1)
                sp.dma_start(a["C_prompt"].rearrange("l b h d v -> (l b d) h v"), C[:, :, 0:DV]).then_inc(s["stored"], 16)
                sp.dma_start(a["n_prompt"].rearrange("l b h d -> (l b d) h").unsqueeze(2), C[:, :, DV:DV + 1],
                             allow_slow_non_contiguous=True).then_inc(s["stored"], 16)
                for b in range(NB):
                    par = b % 2
                    if b >= 2:
                        sp.wait_ge(c_stored[par], 32 * (b // 2))
                    sp.dma_start(CS[:, par, :, 0:DV], C_in[b]).then_inc(c_landed[par], 16)
                    sp.dma_start(CS[:, par, :, DV:DV + 1], n_in[b].unsqueeze(2),
                                 allow_slow_non_contiguous=True).then_inc(c_landed[par], 16)
                    if b >= 1:
                        store_state(sp, b - 1)
                store_state(sp, NB - 1)
                sp.wait_ge(s["stored"], 32)
                for par in range(2):
                    sp.wait_ge(c_stored[par], 32 * (NB // 2))

            @block.tensor
            def _(pe):
                def turns(c, half, par):
                    sample = isinstance(c, int) and c == NC
                    n = TS if sample else L
                    x = inp[:, par, :, :]
                    pe.wait_ge(landed[par], half * 16 + 16)
                    pe.wait_ge(s["state_added"], c + 1)
                    for h in range(H):
                        mm = pe.transpose(ps[0:n, 0, h * L:(h + 1) * L], x[:, 4 + h, 0:n], g.ident[:, :])
                    mm.then_inc(s["k_turned"], 1)
                    for j in range(8):
                        mm = pe.transpose(ps[0:n, 1 + j // 4, (j % 4) * P:(j % 4 + 1) * P], x[:, 8 + j, 0:n],
                                          g.ident[:, :])
                    mm.then_inc(s["v_turned"], 1)
                    for h in range(H):
                        mm = pe.matmul(ps[0:n, 3, h * L:h * L + n], x[:, 4 + h, 0:n], x[:, h, 0:n],
                                       start=True, stop=True)
                    mm.then_inc(s["s_ready"], 1)

                def decays(c):
                    n = TS if isinstance(c, int) and c == NC else L
                    wait(pe, s["yn_ready"], c)
                    for h in range(H):
                        mm = pe.matmul(ps[:, 4, h * L:h * L + n], g.sel[:, h, :], m.U[:, ds(c * L, n)],
                                       start=True, stop=True)
                    mm.then_inc(s["u_ready"], 1)

                def state_weights(c):
                    n = TS if isinstance(c, int) and c == NC else L
                    for h in range(H):
                        mm = pe.matmul(ps[:, 5, h * L:h * L + n], g.sel[:, h, :], m.WI[:, ds(c * L, n)],
                                       start=True, stop=True)
                    mm.then_inc(s["wi_ready"], 1)

                def turn_y(c):
                    n = TS if isinstance(c, int) and c == NC else L
                    pe.wait_ge(s["yn_ready"], c + 1)
                    for j in range(8):
                        mm = pe.transpose(ps[:, 6 + j // 4, (j % 4) * L:(j % 4) * L + n],
                                          YN[0:n, j // 2, (j % 2) * P:(j % 2 + 1) * P], g.ident[0:n, 0:n])
                    mm.then_inc(s["y_turned"], 1)

                def ahead(c, half, par):
                    turns(c, half, par)
                    decays(c)
                    state_weights(c)

                def chunk(c, par, ahead_of):
                    wait(pe, s["y_gated"], c)
                    pe.wait_ge(s["q_scaled"], c + 1)
                    pe.wait_ge(s["masked"], c + 1)
                    pe.wait_ge(s["scores_ready"], c + 1)
                    pe.wait_ge(s["v_copied"], c + 1)
                    for h in range(H):
                        pe.matmul(ps[:, 4 + h, 0:DV + 1], QW[:, h, :], C[:, h, :], start=True, stop=False)
                        mm = pe.matmul(ps[:, 4 + h, 0:DV + 1], A[:, h, :], VA[:, h, :], start=False, stop=True)
                    mm.then_inc(s["num_ready"], 1)
                    pe.wait_ge(s["k_scaled"], c + 1)
                    for h in range(H):
                        mm = pe.matmul(ps[:, h, 0:DV + 1], KW[:, h, :], VA[:, h, :], start=True, stop=True)
                    mm.then_inc(s["state_ready"], 1)
                    turns(*ahead_of)
                    decays(ahead_of[0])
                    turn_y(c)
                    state_weights(ahead_of[0])

                pe.wait_ge(s["ones_ready"], 1)
                pipelined(pe, ahead, chunk)
                pe.wait_ge(s["y_gated"], NC)
                pe.wait_ge(s["q_scaled"], NC + 1)
                pe.wait_ge(s["masked"], NC + 1)
                pe.wait_ge(s["scores_ready"], NC + 1)
                pe.wait_ge(s["v_copied"], NC + 1)
                pe.wait_ge(s["k_scaled"], NC + 1)
                for h in range(H):
                    pe.matmul(ps[0:TS, 4 + h, 0:DV + 1], A[0:TS, h, 0:TS], VA[0:TS, h, :], start=True, stop=False)
                for b in range(NB):
                    pe.wait_ge(c_landed[b % 2], 32 * (b // 2 + 1))
                    pe.wait_ge(s["qb_ready"], b + 1)
                    for h in range(H):
                        mm = pe.matmul(ps[0:TS, 4 + h, 0:DV + 1], QB[:, b % 2, h, :], CS[:, b % 2, h, :],
                                       start=False, stop=(b == NB - 1))
                    mm.then_inc(s["b_inter"], 1)
                    pe.wait_ge(s["kb_ready"], b + 1)
                    wait(pe, s["b_added"], b)
                    for h in range(H):
                        mm = pe.matmul(ps[:, h, 0:DV + 1], KB[:, b % 2, h, :], VA[0:TS, h, :], start=True, stop=True)
                    mm.then_inc(s["b_state"], 1)
                turn_y(NC)

            @block.scalar
            def _(act):
                act.preload_act_table_set("natural_log_exp_and_others")
                def ahead(c, half, par):
                    n = TS if isinstance(c, int) and c == NC else L
                    act.wait_ge(s["k_turned"], c + 1)
                    wait(act, s["state_ready"], c)
                    for h in range(H):
                        ins = act.activation(KW[0:n, h, :], bank(0)[0:n, h, :], ACT.Copy,
                                             scale=m.NAT[0:n, ds(c, 1), 2 * H + h:2 * H + h + 1].rearrange("p a b -> p (a b)"))
                    ins.then_inc(s["k_scaled"], 1)
                    act.wait_ge(s["v_turned"], c + 1)
                    act.activation(VA[0:n, :, 0:DV], ps[0:n, 1:3, :].rearrange("p b (h v) -> p (b h) v", h=2),
                                   ACT.Copy).then_inc(s["v_copied"], 1)
                    act.wait_ge(s["masked"], c + 1)
                    for h in range(H):
                        ins = act.activation(E[0:n, h, 0:n], E[0:n, h, 0:n], ACT.Exp,
                                             bias=m.NAT[0:n, ds(c, 1), h:h + 1].rearrange("p a b -> p (a b)"))
                    ins.then_inc(s["decays_ready"], 1)

                def squares(c):
                    n = TS if isinstance(c, int) and c == NC else L
                    act.wait_ge(s["small_steps"], c * 7 + 4)
                    for h in range(H):
                        ins = act.activation(YN[0:n, h, :], ps[0:n, 4 + h, 0:DV], ACT.Square,
                                             scale=SM[0:n, 2, h:h + 1], accum_out=SM[0:n, 3, h:h + 1])
                    ins.then_inc(s["sq_ready"], 1)
                    act.wait_ge(s["sq_ready"], c + 1)
                    act.activation(SM[0:n, 4, :], SM[0:n, 3, :], ACT.Ln, bias=g.eps[0:n, 0:1], scale=1.0 / DV
                                   ).then_inc(s["ln_ready"], 1)
                    act.wait_ge(s["ln_ready"], c + 1)
                    act.activation(SM[0:n, 5, :], SM[0:n, 4, :], ACT.Exp, scale=-0.5).then_inc(s["est_ready"], 1)

                def high(c):
                    n = TS if isinstance(c, int) and c == NC else L
                    act.wait_ge(s["y_gated"], c + 1)
                    act.activation(g.HH[:, :, ds(c * L, n)], TT[:, :, 0:n], ACT.Copy).then_inc(s["hi_ready"], 1)

                def chunk(c, par, ahead_of):
                    squares(c)
                    ahead(*ahead_of)
                    high(c)
                pipelined(act, ahead, chunk)
                squares(NC)
                high(NC)

            @block.vector
            def _(dve):
                def ahead(c, half, par):
                    sample = isinstance(c, int) and c == NC
                    n = TS if sample else L
                    mk = mask8 if sample else mask
                    dve.wait_ge(s["u_ready"], c + 1)
                    wait(dve, s["scores_ready"], c)
                    dve.tensor_tensor(E[0:n, :, 0:n], bank(4, n)[0:n], mk[:, :].unsqueeze(1).to_broadcast([n, H, n]),
                                      ALU.add).then_inc(s["masked"], 1)
                    dve.wait_ge(s["wi_ready"], c + 1)
                    wait(dve, s["num_ready"], c)
                    dve.tensor_tensor(QW[:, :, 0:n], inp[:, par, 0:H, 0:n], bank(5, n), ALU.mult).then_inc(s["q_scaled"], 1)
                    dve.wait_ge(s["s_ready"], c + 1)
                    dve.wait_ge(s["decays_ready"], c + 1)
                    dve.tensor_tensor(A[0:n, :, 0:n], bank(3, n)[0:n], E[0:n, :, 0:n], ALU.mult).then_inc(s["scores_ready"], 1)

                def denominator(c):
                    n = TS if isinstance(c, int) and c == NC else L
                    base = c * 7
                    if not (isinstance(c, int) and c == NC):
                        dve.wait_ge(s["num_ready"], c + 1)
                    den = ps[0:n, 4:8, DV:DV + 1].rearrange("p h o -> p (h o)")
                    dve.tensor_copy(SM[0:n, 0, :], den).then_inc(s["small_steps"], 1)
                    dve.wait_ge(s["small_steps"], base + 1)
                    dve.scalar_tensor_tensor(SM[0:n, 1, :], SM[0:n, 0, :], -1.0, SM[0:n, 0, :], ALU.mult, ALU.max
                                             ).then_inc(s["small_steps"], 1)
                    dve.wait_ge(s["small_steps"], base + 2)
                    dve.tensor_tensor(SM[0:n, 1, :], SM[0:n, 1, :],
                                      m.NAT[0:n, ds(c, 1), H:2 * H].rearrange("p a b -> p (a b)"), ALU.max
                                      ).then_inc(s["small_steps"], 1)
                    dve.wait_ge(s["small_steps"], base + 3)
                    dve.reciprocal(SM[0:n, 2, :], SM[0:n, 1, :]).then_inc(s["small_steps"], 1)

                def normed(c):
                    n = TS if isinstance(c, int) and c == NC else L
                    base = c * 7
                    dve.wait_ge(s["est_ready"], c + 1)
                    dve.tensor_scalar(SM[0:n, 3, :], SM[0:n, 3, :], 1.0 / DV, EPS, ALU.mult, ALU.add
                                      ).then_inc(s["small_steps"], 1)
                    dve.scalar_tensor_tensor(SM[0:n, 6, :], SM[0:n, 5, :], -0.5, SM[0:n, 5, :], ALU.mult, ALU.mult
                                             ).then_inc(s["small_steps"], 1)
                    dve.wait_ge(s["small_steps"], base + 6)
                    dve.tensor_tensor(SM[0:n, 6, :], SM[0:n, 6, :], SM[0:n, 3, :], ALU.mult).then_inc(s["small_steps"], 1)
                    dve.wait_ge(s["small_steps"], base + 7)
                    dve.scalar_tensor_tensor(SM[0:n, 6, :], SM[0:n, 6, :], 1.5, SM[0:n, 5, :], ALU.add, ALU.mult
                                             ).then_inc(s["newton_done"], 1)
                    dve.wait_ge(s["newton_done"], c + 1)
                    dve.tensor_tensor(SM[0:n, 7, :], SM[0:n, 6, :], SM[0:n, 2, :], ALU.mult).then_inc(s["scale_ready"], 1)
                    dve.wait_ge(s["scale_ready"], c + 1)
                    for h in range(H):
                        ins = dve.tensor_scalar(YN[0:n, h, :], ps[0:n, 4 + h, 0:DV], SM[0:n, 7, h:h + 1], None, ALU.mult)
                    ins.then_inc(s["yn_ready"], 1)

                def state(c):
                    dve.wait_ge(s["state_ready"], c + 1)
                    for h in range(H):
                        ins = dve.scalar_tensor_tensor(
                            C[:, h, :], C[:, h, :], m.DEC[:, ds(c, 1), h:h + 1].rearrange("p a b -> p (a b)"),
                            ps[:, h, 0:DV + 1], ALU.mult, ALU.add)
                    ins.then_inc(s["state_added"], 1)

                def gated(c, par):
                    n = TS if isinstance(c, int) and c == NC else L
                    dve.wait_ge(s["y_turned"], c + 1)
                    wait(dve, s["lo_ready"], c)
                    dve.tensor_tensor(TT[:, :, 0:n], ps[:, 6:8, :].rearrange("p b (j t) -> p (b j) t", j=4)[:, :, 0:n],
                                      inp[:, par, 16:24, 0:n], ALU.mult).then_inc(s["y_gated"], 1)

                def chunk(c, par, ahead_of):
                    denominator(c)
                    state(c)
                    normed(c)
                    ahead(*ahead_of)
                    gated(c, par)

                dve.memset(C[:, :, :], 0.0).then_inc(s["state_added"], 1)
                dve.memset(VA[:, :, DV:DV + 1], 1.0).then_inc(s["ones_ready"], 1)
                dve.wait_ge(s["consts"], 64)
                pipelined(dve, ahead, chunk)
                for b in range(NB):
                    wait(dve, s["b_inter"], b - 1)
                    dve.wait_ge(s["q_scaled"], NC + 1)
                    dve.tensor_tensor(QB[:, b % 2, :, :], QW[:, :, 0:TS],
                                      bm[:, b, :].unsqueeze(1).to_broadcast([P, H, TS]), ALU.mult).then_inc(s["qb_ready"], 1)
                    wait(dve, s["b_state"], b - 1)
                    dve.wait_ge(s["k_scaled"], NC + 1)
                    dve.tensor_scalar(KB[:, b % 2, :, :], KW[0:TS, :, :], bmr[:, b:b + 1], None, ALU.mult
                                      ).then_inc(s["kb_ready"], 1)
                    dve.wait_ge(s["b_state"], b + 1)
                    dve.wait_ge(s["b_inter"], b + 1)
                    for h in range(H):
                        ins = dve.scalar_tensor_tensor(CS[:, b % 2, h, :], CS[:, b % 2, h, :],
                                                       m.DEC[:, NC + b, h:h + 1], ps[:, h, 0:DV + 1], ALU.mult, ALU.add)
                    ins.then_inc(s["b_added"], 1)
                denominator(NC)
                normed(NC)
                gated(NC, 0)

            @block.gpsimd
            def _(pool):
                def low(c):
                    n = TS if isinstance(c, int) and c == NC else L
                    pool.wait_ge(s["hi_ready"], c + 1)
                    pool.tensor_tensor(g.HL[:, :, ds(c * L, n)], TT[:, :, 0:n],
                                       g.HH[:, :, ds(c * L, n)].bitcast(F32), ALU.subtract).then_inc(s["lo_ready"], 1)
                low(0)
                low(1)
                with pool.Fori(1, NC // 2) as i:
                    for par in range(2):
                        low(i * 2 + par)
                low(NC)


def gates_gla(nc, g, tag, a, GP):
    with Scope(nc, tag) as sc:
        W2 = sc.sb("w_gate2", [16, H * DQK])
        T1 = sc.sb("softplus", [P, TP])
        ZM = sc.sb("z_min", [P, TP])
        B = sc.sb("b", [P, 2, TP])
        s_in, s_z, s_a, s_m, s_d, s_b = (sc.sem(n) for n in (
            "w_landed", "z_ready", "act_steps", "z_min_ready", "log_ready", "summed"))
        s_out = [sc.sem("stored0"), sc.sem("stored1")]
        with nc.Block() as block:
            @block.sync
            def _(sp):
                sp.dma_start(W2[:, :], a["w_gate2_gla"][0]).then_inc(s_in, 16)
                for h in range(H):
                    sp.wait_ge(s_b, h + 1)
                    sp.dma_start(g.PT[24 + h, :, :], B[:, h % 2, :]).then_inc(s_out[h % 2], 16)
                for par in range(2):
                    sp.wait_ge(s_out[par], 32)

            @block.tensor
            def _(pe):
                pe.wait_ge(s_in, 16)
                for h in range(H):
                    b0 = 3 * (h % 2)
                    if h >= 2:
                        pe.wait_ge(s_a, 3 * (h - 2) + 1)
                        pe.wait_ge(s_m, h - 1)
                    for t in range(GRP):
                        mm = pe.matmul(g.ps[:, b0 + t, 0:GT], W2[:, h * DQK:(h + 1) * DQK],
                                       GP[0:16, t * GT:(t + 1) * GT], start=True, stop=True)
                    mm.then_inc(s_z, 1)

            @block.scalar
            def _(act):
                act.preload_act_table_set("natural_log_exp_and_others")
                for h in range(H):
                    b0 = 3 * (h % 2)
                    act.wait_ge(s_m, h + 1)
                    wait(act, s_d, h)
                    act.activation(by_group(T1[:, :]), g.ps[:, b0:b0 + 3, 0:GT], ACT.Abs,
                                   bias=g.vec[:, V_BGATE + h:V_BGATE + h + 1]).then_inc(s_a, 1)
                    act.wait_ge(s_a, 3 * h + 1)
                    act.activation(T1[:, :], T1[:, :], ACT.Exp, scale=-1.0).then_inc(s_a, 1)
                    act.wait_ge(s_a, 3 * h + 2)
                    act.activation(T1[:, :], T1[:, :], ACT.Ln, bias=1.0).then_inc(s_a, 1)

            @block.vector
            def _(dve):
                for h in range(H):
                    b0 = 3 * (h % 2)
                    dve.wait_ge(s_z, h + 1)
                    wait(dve, s_b, h)
                    dve.tensor_scalar(by_group(ZM[:, :]), g.ps[:, b0:b0 + 3, 0:GT],
                                      g.vec[:, V_BGATE + h:V_BGATE + h + 1], 0.0, ALU.add, ALU.min).then_inc(s_m, 1)
                    dve.wait_ge(s_a, 3 * h + 3)
                    dve.wait_ge(s_m, h + 1)
                    dve.tensor_tensor(ZM[:, :], ZM[:, :], T1[:, :], ALU.subtract).then_inc(s_d, 1)
                    dve.wait_ge(s_d, h + 1)
                    if h >= 2:
                        dve.wait_ge(s_out[h % 2], 16)
                    dve.tensor_tensor_scan(B[:, h % 2, :], g.reset[:, :], ZM[:, :], 0.0, ALU.mult, ALU.add
                                           ).then_inc(s_b, 1)


LEVELS = (64, 32, 16, 8, 4, 2, 1)
ITAU = 1.0 / 16.0


def gla_mix(nc, g, tag, a):
    NLV = len(LEVELS)
    with Scope(nc, tag) as sc:
        inp = sc.sb("qkvb", [P, 2, 20, L])
        gate = sc.sb("gate", [P, 2, D // P, L])
        XL = sc.sb("levels", [P, NLV, H, L])
        EBs = sc.sb("exp_b", [P, 2, H, L])
        QEs = sc.sb("q_decayed", [P, 2, H, L])
        CS = sc.sb("sample_state", [P, 2, H, DV])
        KD = sc.sb("k_decayed", [P, H, L])
        VN = sc.sb("v", [P, H, DV])
        S = sc.sb("state", [P, H, DV])
        YN = sc.sb("y_normed", [P, H, DV])
        TT = sc.sb("y_gated", [P, D // P, L])
        SM = sc.sb("small", [P, 8, H])
        masks = sc.sb("masks", [P, NLV + 1, L], U32)
        bmr = sc.sb("batch_rows", [TS, NB])
        A = cheads(g.wst[:, 0, 0:512])
        KN = cheads(g.wst[:, 0, 512:1024])
        bm = g.wst[:, 1, 0:512].rearrange("p (b t) -> p b t", b=NB)
        free = XL[:, :, :, :].rearrange("p v h t -> p (v h t)")
        QB = free[:, 2048:2560].rearrange("p (b h t) -> p b h t", b=2, h=H)
        KB = free[0:TS, 2560:3584].rearrange("p (b h d) -> p b h d", b=2, h=H)
        s = {name: sc.sem(name) for name in ("consts", "args_ready", "kd_arg_ready", "level_exps_ready", "b_exps_ready", "kd_exp_ready",
                         "levels_ready", "q_ready", "k_ready", "k_turned", "k_copied", "v_turned", "v_copied",
                         "level_done", "level_merged", "merge_begun", "num_ready", "sq_ready", "ln_ready", "est_ready",
                         "small_steps", "yn_ready", "state_ready", "state_added", "y_turned", "y_gated",
                         "hi_ready", "lo_ready", "stored", "cleared", "qb_ready", "kb_ready", "b_inter",
                         "b_state", "b_added")}
        landed = [sc.sem("landed0"), sc.sem("landed1")]
        gate_landed = [sc.sem("gate_landed0"), sc.sem("gate_landed1")]
        c_landed = [sc.sem("c_landed0"), sc.sem("c_landed1")]
        c_stored = [sc.sem("c_stored0"), sc.sem("c_stored1")]
        ps = g.ps
        sample = lambda c: isinstance(c, int) and c == NC
        size = lambda c: TS if sample(c) else L
        bank = lambda b, n=L: ps[:, b, :].rearrange("p (h t) -> p h t", h=H)[:, :, 0:n]
        S_in = a["state_gla_S"].rearrange("l b h d v -> (l b) d h v")
        S_out = a["S_sample"].rearrange("l b h d v -> (l b) d h v")
        levels_of = lambda c: range(4 if sample(c) else 0, NLV + 1)

        def halves(ap, n, half):
            return ap.rearrange("p h (b u t) -> p h b u t", u=2, t=n)[:, :, :, half, :]

        def store_state(sp, b):
            sp.wait_ge(s["b_added"], b + 1)
            sp.dma_start(S_out[b], CS[:, b % 2, :, :]).then_inc(c_stored[b % 2], 16)

        def levels_base(c):
            return NLV * NC if sample(c) else c * NLV

        def merges_base(c):
            return (NLV + 1) * NC if sample(c) else c * (NLV + 1)

        def pipelined(eng, prepare, ahead, chunk):
            prepare(0, 0, 0)
            ahead(0, 0, 0)
            prepare(1, 0, 1)
            chunk(0, 0, (1, 0, 1), (2, 1, 0))
            chunk(1, 1, (2, 1, 0), (3, 1, 1))
            with eng.Fori(1, NC // 2 - 1) as i:
                chunk(i * 2, 0, (i * 2 + 1, i, 1), (i * 2 + 2, i + 1, 0))
                chunk(i * 2 + 1, 1, (i * 2 + 2, i + 1, 0), (i * 2 + 3, i + 1, 1))
            chunk(NC - 2, 0, (NC - 1, NC // 2 - 1, 1), (NC, NC // 2, 0))
            chunk(NC - 1, 1, (NC, NC // 2, 0), None)

        with nc.Block() as block:
            @block.sync
            def _(sp):
                sp.dma_start(masks[:, :, :], a["c_levels"]).then_inc(s["consts"], 16)
                sp.dma_start(bm, a["c_batch_cols"]).then_inc(s["consts"], 16)
                sp.dma_start(bmr[:, :], a["c_batch_rows"]).then_inc(s["consts"], 16)

                def load(c, half, par):
                    n = size(c)
                    if half is not None:
                        sp.wait_ge(s["level_merged"], (NLV + 1) * (NC - 1) if sample(c) else (c - 1) * (NLV + 1))
                        sp.wait_ge(s["q_ready"], c - 1)
                    for rows, at in ((slice(0, 16), 0), (slice(24, 28), 16)):
                        sp.dma_start(inp[:, par, at:at + rows.stop - rows.start, 0:n],
                                     g.PT[rows, :, ds(c * L, n)].rearrange("m p t -> p m t")
                                     ).then_inc(landed[par], 16)
                    if half is not None:
                        sp.wait_ge(s["y_gated"], c - 1)
                    sp.dma_start(gate[:, par, :, 0:n], g.PT[16:24, :, ds(c * L, n)].rearrange("m p t -> p m t")
                                 ).then_inc(gate_landed[par], 16)
                load(0, None, 0)
                load(1, None, 1)
                for b in range(2):
                    sp.dma_start(CS[:, b, :, :], S_in[b]).then_inc(c_landed[b], 16)
                with sp.Fori(1, NC // 2) as i:
                    for par in range(2):
                        load(i * 2 + par, i, par)
                load(NC, NC // 2, 0)
                sp.wait_ge(s["state_added"], NC + 1)
                sp.dma_start(a["S_prompt"].rearrange("l b h d v -> (l b d) h v"), S[:, :, :]).then_inc(s["stored"], 16)
                for b in range(NB):
                    store_state(sp, b)
                    if b + 2 < NB:
                        sp.wait_ge(c_stored[b % 2], 16 * (b // 2 + 1))
                        sp.dma_start(CS[:, b % 2, :, :], S_in[b + 2]).then_inc(c_landed[b % 2], 16)
                sp.wait_ge(s["stored"], 16)
                for par in range(2):
                    sp.wait_ge(c_stored[par], 16 * (NB // 2))

            @block.gpsimd
            def _(pool):
                def prepare(c, half, par):
                    n = size(c)
                    Bc = inp[:, par, 16:20, 0:n]
                    pool.wait_ge(landed[par], half * 32 + 32)
                    for v in levels_of(c):
                        if v == NLV:
                            continue
                        w = LEVELS[v]
                        nb = n // (2 * w)
                        if not (isinstance(c, int) and c == 0):
                            last = (NC - 1) * (NLV + 1) if sample(c) else (c - 1) * (NLV + 1)
                            pool.wait_ge(s["level_done"], last + (v + 1))
                        mid = Bc.rearrange("p h (b u) -> p h b u", u=2 * w)[:, :, :, w - 1:w].to_broadcast([P, H, nb, w])
                        pool.tensor_tensor(halves(XL[:, v, :, 0:n], w, 0), mid, halves(Bc, w, 0), ALU.subtract)
                        pool.tensor_tensor(halves(XL[:, v, :, 0:n], w, 1), halves(Bc, w, 1), mid, ALU.subtract
                                           ).then_inc(s["args_ready"], 1)
                    wait(pool, s["k_turned"], c)
                    blk = DS if sample(c) else L
                    end = Bc.rearrange("p h (b u) -> p h b u", u=blk)
                    pool.tensor_tensor(KD[:, :, 0:n].rearrange("p h (b u) -> p h b u", u=blk),
                                       end[:, :, :, blk - 1:blk].to_broadcast([P, H, n // blk, blk]), end,
                                       ALU.subtract).then_inc(s["kd_arg_ready"], 1)

                def low(c):
                    n = size(c)
                    pool.wait_ge(s["hi_ready"], c + 1)
                    pool.tensor_tensor(g.HL[:, :, ds(c * L, n)], TT[:, :, 0:n],
                                       g.HH[:, :, ds(c * L, n)].bitcast(F32), ALU.subtract).then_inc(s["lo_ready"], 1)

                def chunk(c, par, ahead_of, prepare_for):
                    if prepare_for:
                        prepare(*prepare_for)
                    low(c)
                pipelined(pool, prepare, lambda *c: None, chunk)
                low(NC)

            @block.scalar
            def _(act):
                act.preload_act_table_set("natural_log_exp_and_others")
                def prepare(c, half, par):
                    n = size(c)
                    act.wait_ge(landed[par], half * 32 + 32)
                    for v in levels_of(c):
                        if v == NLV:
                            continue
                        act.wait_ge(s["args_ready"], levels_base(c) + (v + 1 - levels_of(c)[0]))
                        act.activation(XL[:, v, :, 0:n], XL[:, v, :, 0:n], ACT.Exp, scale=ITAU
                                       ).then_inc(s["level_exps_ready"], 1)
                    if isinstance(c, int) and c < 2:
                        pass
                    else:
                        act.wait_ge(s["state_added"], c)
                    act.activation(EBs[:, par, :, 0:n], inp[:, par, 16:20, 0:n], ACT.Exp, scale=ITAU
                                   ).then_inc(s["b_exps_ready"], 1)
                    act.wait_ge(s["kd_arg_ready"], c + 1)
                    act.activation(KD[:, :, 0:n], KD[:, :, 0:n], ACT.Exp, scale=ITAU).then_inc(s["kd_exp_ready"], 1)

                def ahead(c, half, par):
                    n = size(c)
                    act.wait_ge(s["v_turned"], c + 1)
                    act.activation(VN[0:n, :, :], ps[0:n, 1:3, :].rearrange("p b (h v) -> p (b h) v", h=2),
                                   ACT.Copy).then_inc(s["v_copied"], 1)
                    act.wait_ge(s["k_turned"], c + 1)
                    act.activation(KN[0:n, :, :], bank(0)[0:n], ACT.Copy).then_inc(s["k_copied"], 1)

                def squares(c):
                    n = size(c)
                    act.wait_ge(s["b_inter"] if sample(c) else s["num_ready"], NB if sample(c) else c + 1)
                    wait(act, s["y_turned"], c)
                    for h in range(H):
                        ins = act.activation(YN[0:n, h, :], ps[0:n, 4 + h, 0:DV], ACT.Square,
                                             accum_out=SM[0:n, 3, h:h + 1])
                    ins.then_inc(s["sq_ready"], 1)
                    act.wait_ge(s["sq_ready"], c + 1)
                    act.activation(SM[0:n, 4, :], SM[0:n, 3, :], ACT.Ln, bias=g.eps[0:n, 0:1], scale=1.0 / DV
                                   ).then_inc(s["ln_ready"], 1)
                    act.wait_ge(s["ln_ready"], c + 1)
                    act.activation(SM[0:n, 5, :], SM[0:n, 4, :], ACT.Exp, scale=-0.5).then_inc(s["est_ready"], 1)

                def high(c):
                    n = size(c)
                    act.wait_ge(s["y_gated"], c + 1)
                    act.activation(g.HH[:, :, ds(c * L, n)], TT[:, :, 0:n], ACT.Copy).then_inc(s["hi_ready"], 1)

                def chunk(c, par, ahead_of, prepare_for):
                    squares(c)
                    ahead(*ahead_of)
                    if prepare_for:
                        prepare(*prepare_for)
                    high(c)
                pipelined(act, prepare, ahead, chunk)
                squares(NC)
                high(NC)

            @block.vector
            def _(dve):
                def prepare(c, half, par):
                    n = size(c)
                    q, k = inp[:, par, 0:H, 0:n], inp[:, par, H:2 * H, 0:n]
                    for v in levels_of(c):
                        if v == NLV:
                            continue
                        dve.wait_ge(s["level_exps_ready"], levels_base(c) + (v + 1 - levels_of(c)[0]))
                        for half_, x in ((0, k), (1, q)):
                            dst = halves(XL[:, v, :, 0:n], LEVELS[v], half_)
                            ins = dve.tensor_tensor(dst, dst, halves(x, LEVELS[v], half_), ALU.mult)
                        ins.then_inc(s["levels_ready"], 1)
                    dve.wait_ge(s["b_exps_ready"], c + 1)
                    if not (isinstance(c, int) and c < 2):
                        dve.wait_ge(s["num_ready"], c - 1)
                    dve.tensor_tensor(QEs[:, par, :, 0:n], EBs[:, par, :, 0:n], q, ALU.mult).then_inc(s["q_ready"], 1)
                    dve.wait_ge(s["kd_exp_ready"], c + 1)
                    dve.tensor_tensor(KD[:, :, 0:n], KD[:, :, 0:n], k, ALU.mult).then_inc(s["k_ready"], 1)

                def merge(c, first, last):
                    n = size(c)
                    for j, v in enumerate(levels_of(c)):
                        if not first <= j < last:
                            continue
                        done = merges_base(c) + (j + 1)
                        dve.wait_ge(s["level_done"], done)
                        if j == 0:
                            wait(dve, s["num_ready"], c)
                        if j or not (isinstance(c, int) and c == 0):
                            dve.wait_ge(s["level_merged"], done - 1)
                        dve.sem_inc(s["merge_begun"], 1)
                        dve.copy_predicated(A[0:n, :, 0:n], masks[0:n, v, 0:n].unsqueeze(1).to_broadcast([n, H, n]),
                                            bank((3 + j) % 4, n)[0:n]).then_inc(s["level_merged"], 1)

                def ahead(c, half, par):
                    merge(c, 0, NLV + 1)

                def normed(c):
                    n = size(c)
                    base = c * 4
                    dve.wait_ge(s["est_ready"], c + 1)
                    dve.tensor_scalar(SM[0:n, 6, :], SM[0:n, 3, :], 1.0 / DV, EPS, ALU.mult, ALU.add
                                      ).then_inc(s["small_steps"], 1)
                    dve.scalar_tensor_tensor(SM[0:n, 7, :], SM[0:n, 5, :], -0.5, SM[0:n, 5, :], ALU.mult, ALU.mult
                                             ).then_inc(s["small_steps"], 1)
                    dve.wait_ge(s["small_steps"], base + 2)
                    dve.tensor_tensor(SM[0:n, 6, :], SM[0:n, 7, :], SM[0:n, 6, :], ALU.mult).then_inc(s["small_steps"], 1)
                    dve.wait_ge(s["small_steps"], base + 3)
                    dve.scalar_tensor_tensor(SM[0:n, 7, :], SM[0:n, 6, :], 1.5, SM[0:n, 5, :], ALU.add, ALU.mult
                                             ).then_inc(s["small_steps"], 1)
                    dve.wait_ge(s["small_steps"], base + 4)
                    for h in range(H):
                        ins = dve.tensor_scalar(YN[0:n, h, :], ps[0:n, 4 + h, 0:DV], SM[0:n, 7, h:h + 1], None, ALU.mult)
                    ins.then_inc(s["yn_ready"], 1)

                def state(c, par):
                    dve.wait_ge(s["state_ready"], c + 1)
                    for h in range(H):
                        ins = dve.scalar_tensor_tensor(S[:, h, :], S[:, h, :], EBs[:, par, h, L - 1:L], ps[:, h, 0:DV],
                                                       ALU.mult, ALU.add)
                    ins.then_inc(s["state_added"], 1)

                def gated(c, par):
                    n = size(c)
                    dve.wait_ge(s["y_turned"], c + 1)
                    wait(dve, s["lo_ready"], c)
                    dve.wait_ge(gate_landed[par], c * 8 + (16 if par == 0 else 8))
                    dve.tensor_tensor(TT[:, :, 0:n], ps[:, 4:6, :].rearrange("p b (j t) -> p (b j) t", j=4)[:, :, 0:n],
                                      gate[:, par, :, 0:n], ALU.mult).then_inc(s["y_gated"], 1)

                def chunk(c, par, ahead_of, prepare_for):
                    state(c, par)
                    normed(c)
                    if sample(ahead_of[0]):
                        dve.wait_ge(s["num_ready"], NC)
                        dve.memset(A, 0.0).then_inc(s["cleared"], 1)
                        dve.wait_ge(s["cleared"], 2)
                    merge(ahead_of[0], 0, 4)
                    gated(c, par)
                    merge(ahead_of[0], 4, NLV + 1)
                    if prepare_for:
                        prepare(*prepare_for)

                dve.memset(S[:, :, :], 0.0).then_inc(s["state_added"], 1)
                dve.memset(A, 0.0).then_inc(s["cleared"], 1)
                dve.wait_ge(s["cleared"], 1)
                dve.wait_ge(s["consts"], 48)
                pipelined(dve, prepare, ahead, chunk)
                for b in range(NB):
                    wait(dve, s["b_inter"], b - 1)
                    dve.wait_ge(s["level_done"], (NLV + 1) * NC + 4)
                    dve.wait_ge(s["q_ready"], NC + 1)
                    dve.tensor_tensor(QB[:, b % 2, :, :], QEs[:, 0, :, 0:TS],
                                      bm[:, b, :].unsqueeze(1).to_broadcast([P, H, TS]), ALU.mult).then_inc(s["qb_ready"], 1)
                    wait(dve, s["b_state"], b - 1)
                    dve.wait_ge(s["k_copied"], NC + 1)
                    dve.tensor_scalar(KB[:, b % 2, :, :], KN[0:TS, :, :], bmr[:, b:b + 1], None, ALU.mult
                                      ).then_inc(s["kb_ready"], 1)
                    dve.wait_ge(s["b_state"], b + 1)
                    dve.wait_ge(s["b_inter"], b + 1)
                    for h in range(H):
                        t = b * DS + DS - 1
                        ins = dve.scalar_tensor_tensor(CS[:, b % 2, h, :], CS[:, b % 2, h, :],
                                                       EBs[:, 0, h, t:t + 1], ps[:, h, 0:DV], ALU.mult, ALU.add)
                    ins.then_inc(s["b_added"], 1)
                normed(NC)
                gated(NC, 0)

            @block.tensor
            def _(pe):
                def turns(c, half, par):
                    n = size(c)
                    x = inp[:, par, :, :]
                    pe.wait_ge(landed[par], half * 32 + 32)
                    pe.wait_ge(s["state_added"], c + 1)
                    for j in range(8):
                        mm = pe.transpose(ps[0:n, 1 + j // 4, (j % 4) * P:(j % 4 + 1) * P], x[:, 8 + j, 0:n],
                                          g.ident[:, :])
                    mm.then_inc(s["v_turned"], 1)
                    pe.wait_ge(s["k_ready"], c + 1)
                    for h in range(H):
                        mm = pe.transpose(ps[0:n, 0, h * L:(h + 1) * L], KD[:, h, 0:n], g.ident[:, :])
                    mm.then_inc(s["k_turned"], 1)

                def levels(c, par, first, last):
                    n = size(c)
                    x = inp[:, par, :, :]
                    for j, v in enumerate(levels_of(c)):
                        if not first <= j < last:
                            continue
                        if v < NLV:
                            pe.wait_ge(s["levels_ready"], levels_base(c) + (j + 1))
                        if j == 1:
                            pe.wait_ge(s["k_copied"], c + 1)
                        if j == 2:
                            pe.wait_ge(s["v_copied"], c + 1)
                        if j >= 4:
                            pe.wait_ge(s["level_merged"], merges_base(c) + (j - 3))
                        for h in range(H):
                            lhs, rhs = (XL[:, v, h, 0:n],) * 2 if v < NLV else (x[:, H + h, 0:n], x[:, h, 0:n])
                            mm = pe.matmul(ps[0:n, (3 + j) % 4, h * L:h * L + n], lhs, rhs, start=True, stop=True)
                        mm.then_inc(s["level_done"], 1)

                def ahead(c, half, par):
                    turns(c, half, par)
                    levels(c, par, 0, NLV + 1)

                def turn_y(c):
                    n = size(c)
                    pe.wait_ge(s["yn_ready"], c + 1)
                    for j in range(8):
                        mm = pe.transpose(ps[:, 4 + j // 4, (j % 4) * L:(j % 4) * L + n],
                                          YN[0:n, j // 2, (j % 2) * P:(j % 2 + 1) * P], g.ident[0:n, 0:n])
                    mm.then_inc(s["y_turned"], 1)

                def chunk(c, par, ahead_of, prepare_for):
                    wait(pe, s["y_gated"], c)
                    pe.wait_ge(s["q_ready"], c + 1)
                    pe.wait_ge(s["v_copied"], c + 1)
                    pe.wait_ge(s["level_merged"], merges_base(c) + (NLV + 1))
                    for h in range(H):
                        pe.matmul(ps[:, 4 + h, 0:DV], QEs[:, par, h, :], S[:, h, :], start=True, stop=False)
                        mm = pe.matmul(ps[:, 4 + h, 0:DV], A[:, h, :], VN[:, h, :], start=False, stop=True)
                    mm.then_inc(s["num_ready"], 1)
                    for h in range(H):
                        mm = pe.matmul(ps[:, h, 0:DV], KN[:, h, :], VN[:, h, :], start=True, stop=True)
                    mm.then_inc(s["state_ready"], 1)
                    turns(*ahead_of)
                    levels(ahead_of[0], ahead_of[2], 0, 4)
                    turn_y(c)
                    levels(ahead_of[0], ahead_of[2], 4, NLV + 1)

                pipelined(pe, lambda *c: None, ahead, chunk)
                pe.wait_ge(s["y_gated"], NC)
                pe.wait_ge(s["level_merged"], merges_base(NC) + 4)
                for h in range(H):
                    pe.matmul(ps[0:TS, 4 + h, 0:DV], A[0:TS, h, 0:TS], VN[0:TS, h, :], start=True, stop=False)
                for b in range(NB):
                    pe.wait_ge(c_landed[b % 2], 16 * (b // 2 + 1))
                    pe.wait_ge(s["qb_ready"], b + 1)
                    for h in range(H):
                        mm = pe.matmul(ps[0:TS, 4 + h, 0:DV], QB[:, b % 2, h, :], CS[:, b % 2, h, :],
                                       start=False, stop=(b == NB - 1))
                    mm.then_inc(s["b_inter"], 1)
                    pe.wait_ge(s["kb_ready"], b + 1)
                    wait(pe, s["b_added"], b)
                    for h in range(H):
                        mm = pe.matmul(ps[:, h, 0:DV], KB[:, b % 2, h, :], VN[0:TS, h, :], start=True, stop=True)
                    mm.then_inc(s["b_state"], 1)
                turn_y(NC)


def mixer_layer(nc, g, a, layer):
    mlstm = layer == 0
    w_in = a["w_in_mlstm"][0] if mlstm else a["w_in_gla"][0]
    wv = w_in.rearrange("(k p) e -> p k e", p=P)
    e0 = 2 * H * DQK + 2 * H * DV
    with Scope(nc, f"m{layer}") as sc:
        m = Globals()
        if mlstm:
            m.U = sc.sb("u", [H, TP])
            m.WI = sc.sb("wi", [H, TP])
            m.NAT = sc.sb("per_token", [P, NC + 1, 3 * H])
            m.DEC = sc.sb("decay", [P, NC + NB, H])
            extra = [(lambda w, k=k, r=r: w[:, k, r:r + H], wv[:, k, e0 + q * H:e0 + (q + 1) * H])
                     for k in range(KD) for q, r in enumerate((0, 32))]
        else:
            extra = [(lambda w: w[:, :, 0:16], wv[:, :, e0:e0 + 16])]
        with Scope(nc, f"g{layer}") as gs:
            GP = gs.sb("extra", [P, TP])
            proj_phase(nc, g, f"p{layer}", a, w_in, (1.0, QK_SCALE) if mlstm else (QK_SCALE, 1.0),
                       ACT.Sigmoid if mlstm else ACT.Silu, V_HEAD_M if mlstm else V_HEAD_G, extra, GP,
                       V_PRE_MIX + KD * layer)
            if mlstm:
                gates_mlstm(nc, g, f"q{layer}", a, GP, m)
            else:
                gates_gla(nc, g, f"q{layer}", a, GP)
        if mlstm:
            mlstm_mix(nc, g, f"x{layer}", a, m)
        else:
            gla_mix(nc, g, f"x{layer}", a)
    with Scope(nc, f"m{layer}y") as sc:
        Y = sc.sb("Y", [P, KD, TP])
        wout_phase(nc, g, f"w{layer}", a["w_out_mlstm"][0] if mlstm else a["w_out_gla"][0], Y)
        post_norm(nc, g, f"qm{layer}", V_POST_MIX + KD * layer, Y)


def build(nc, a, parts):
    g = Globals()
    with ExitStack() as ctx:
        sb = lambda name, shape, dt=F32: ctx.enter_context(nc.sbuf_tensor(name, shape, dt))
        g.ps = ctx.enter_context(nc.psum_tensor("ps", [P, 8, 512], F32))
        g.X = sb("X", [P, KD, TP])
        g.HH = sb("HH", [P, KD, TP], F32R)
        g.HL = sb("HL", [P, KD, TP], F32R)
        g.acc = sb("sum_of_squares", [P, TP])
        g.wst = sb("w_stage", [P, 2, WCOLS])
        g.ident = sb("ident", [P, P])
        g.ones = sb("ones", [P, P])
        g.vec = sb("vec", [P, NVEC])
        g.avg = sb("avg", [P, P])
        g.eps = sb("eps", [P, 1])
        g.reset = sb("reset", [P, TP])
        g.sel = sb("sel", [H, H, L])
        g.negi = sb("negi", [H, H])
        g.PT = nc.dram_tensor("proj_scratch", [28, P, TP], F32, kind="Internal").ap()
        g.const_loads = [(g.reset[:, :], a["c_reset"]), (g.sel[:, :, :], a["c_sel"]), (g.negi[:, :], a["c_negi"]),
                         (g.avg[:, :], a["c_avg"]), (g.eps[:, :], a["c_eps"]),
                         (g.ident[:, :], a["c_ident"]), (g.ones[:, :], a["c_ones"])]
        load_phase(nc, g, a)
        for layer in range(2):
            if f"mix{layer}" in parts:
                mixer_layer(nc, g, a, layer)
            if "ffn" in parts:
                with Scope(nc, f"f{layer}y") as sc:
                    Y = sc.sb("Y", [P, KD, TP])
                    ffn_phase(nc, g, f"f{layer}", layer, a, Y, V_PRE_FFN + KD * layer)
                    post_norm(nc, g, f"qf{layer}", V_POST_FFN + KD * layer, Y, last=layer == 1)
        store_phase(nc, g, a)


PARTS = ("mix0", "mix1", "ffn")
OUTS = [("y_prompt", (1, 1024, 1024)), ("y_sample", (8, 8, 1024)),
        ("C_prompt", (1, 1, 4, 128, 256)), ("n_prompt", (1, 1, 4, 128)), ("m_prompt", (1, 1, 4)),
        ("S_prompt", (1, 1, 4, 128, 256)), ("C_sample", (1, 8, 4, 128, 256)),
        ("n_sample", (1, 8, 4, 128)), ("m_sample", (1, 8, 4)), ("S_sample", (1, 8, 4, 128, 256))]


def constants():
    f = np.float32
    tok = np.arange(L)
    starts = np.ones(TP, f)
    starts[0:SEQ:L] = 0
    starts[SEQ:T:DS] = 0
    heads = np.eye(H, dtype=f)
    s, l = np.arange(L)[:, None], np.arange(L)[None, :]
    after = np.where(s <= l, 0.0, NEG).astype(f)
    s8, l8 = np.arange(TS)[:, None], np.arange(TS)[None, :]
    after8 = np.where((s8 <= l8) & (s8 // DS == l8 // DS), 0.0, NEG).astype(f)
    rows = (np.arange(TS)[:, None] // DS == np.arange(NB)[None, :]).astype(f)
    lv = []
    for w in (64, 32, 16, 8, 4, 2, 1):
        lv.append((s // (2 * w) == l // (2 * w)) & (s % (2 * w) < w) & (l % (2 * w) >= w))
    lv.append(s == l)
    c = {"c_levels": np.stack(lv, 1).astype(np.uint32), "c_reset": np.broadcast_to(starts, (P, TP)).copy(), "c_sel": np.repeat(heads[:, :, None], L, 2),
         "c_negi": -heads, "c_causal": after, "c_causal8": after8, "c_batch_rows": rows,
         "c_batch_cols": np.broadcast_to(rows.T, (P, NB, TS)).copy(),
         "c_ident": np.eye(P, dtype=f), "c_ones": np.ones((P, P), f),
         "c_avg": np.full((P, P), 1.0 / D, f), "c_eps": np.full((P, 1), EPS, f)}
    return c


def wanted(name):
    return name[0] == "y" or (name[0] in "Cnm" and "mix0" in PARTS) or (name[0] == "S" and "mix1" in PARTS)


def kernel(**inputs):
    import concourse.bacc as bacc
    from concourse.bass_utils import run_bass_kernel_spmd as run

    nc = bacc.Bacc("TRN2", target_bir_lowering=False, num_devices=1)
    arrays = {}
    a = {}
    for name, v in list(inputs.items()) + list(constants().items()):
        v = np.ascontiguousarray(v)
        arrays[f"{name}_in"] = v
        a[name] = nc.dram_tensor(f"{name}_in", v.shape, mybir.dt.from_np(v.dtype), kind="ExternalInput").ap()
    for name, shape in OUTS:
        if not wanted(name):
            continue
        a[name] = nc.dram_tensor(f"{name}_out", shape, F32, kind="ExternalOutput").ap()
    build(nc, a, PARTS)
    r = run(nc, [arrays], core_ids=[0])
    return tuple(r.results[0][f"{name}_out"] for name, _ in OUTS if wanted(name))
```
